# Optimizing a Trainium2 kernel written in Bass

```python
import math
import jax, jax.numpy as jnp
from jax import lax
import numpy as np

D_MODEL = 1024
BATCH = 1
SEQ = 256
DEPTH = 1

BRANCH_W = D_MODEL // 2
POOL_WINDOWS = (2, 4, 8, 16)
N_POOL_GROUPS = len(POOL_WINDOWS)
POOL_GROUP_W = BRANCH_W // N_POOL_GROUPS
DILATED_GROUPS = ((128, 1), (512, 4), (2048, 16))
N_ATT_GROUPS = len(DILATED_GROUPS)
HEAD_DIM = 64
HEADS_PER_GROUP = BRANCH_W // HEAD_DIM
N_ATT_HEADS = N_ATT_GROUPS * HEADS_PER_GROUP
QKV_W = N_ATT_HEADS * HEAD_DIM
Q_BLOCK = 128
NUM_BUCKETS = 32
MAX_DISTANCE = 1024
IN_W = 2 * BRANCH_W + 3 * QKV_W + BRANCH_W + 2 * D_MODEL
RMS_EPS = 1e-6
NEG_INF = -1e30


def _rmsnorm(x, g):
    xf = x.astype(jnp.float32)
    r = lax.rsqrt(jnp.mean(xf * xf, axis=-1, keepdims=True) + RMS_EPS)
    return (xf * r).astype(x.dtype) * g

def _t5_bucket(rel):
    nb = NUM_BUCKETS // 2
    ret = (rel > 0).astype(jnp.int32) * nb
    n = jnp.abs(rel)
    max_exact = nb // 2
    nf = jnp.maximum(n, 1).astype(jnp.float32)
    large = max_exact + (jnp.log(nf / max_exact) / math.log(MAX_DISTANCE / max_exact)
                         * (nb - max_exact)).astype(jnp.int32)
    large = jnp.minimum(large, nb - 1)
    return ret + jnp.where(n < max_exact, n, large)

def _multiscale_pool(u, w_pool, pool_scale):
    B, S, _ = u.shape
    ug = u.reshape(B, S, N_POOL_GROUPS, POOL_GROUP_W)
    cs = jnp.cumsum(ug.astype(jnp.float32), axis=1)
    cs = jnp.concatenate([jnp.zeros_like(cs[:, :1]), cs], axis=1)
    pos = jnp.arange(S, dtype=jnp.int32)[:, None]
    half = jnp.array([w // 2 for w in POOL_WINDOWS], dtype=jnp.int32)[None, :]
    lo = jnp.maximum(pos - half, 0)
    hi = jnp.minimum(pos + half - 1, S - 1)
    gidx = jnp.arange(N_POOL_GROUPS, dtype=jnp.int32)[None, :]
    win_sum = cs[:, hi + 1, gidx] - cs[:, lo, gidx]
    count = (hi - lo + 1).astype(jnp.float32)[None, :, :, None]
    pooled = (win_sum / count).astype(u.dtype) - ug
    mixed = jnp.einsum('bsgc,gcd->bsgd', pooled, w_pool)
    return mixed.reshape(B, S, BRANCH_W) * pool_scale

def _dilated_attention(q, k, v, rel_bias):
    B, S = q.shape[0], q.shape[1]
    n_blocks = S // Q_BLOCK
    scale = 1.0 / math.sqrt(HEAD_DIM)
    cfg = []
    for g, (window, dil) in enumerate(DILATED_GROUPS):
        n_side = window // (2 * dil)
        offs = jnp.arange(-n_side, n_side + 1, dtype=jnp.int32) * dil
        bias = rel_bias[_t5_bucket(offs)][:, g * HEADS_PER_GROUP:(g + 1) * HEADS_PER_GROUP]
        cfg.append((offs, bias.T.astype(jnp.float32), k[:, :, g], v[:, :, g]))

    def block(i):
        s0 = i * Q_BLOCK
        qpos = s0 + jnp.arange(Q_BLOCK, dtype=jnp.int32)
        qb = lax.dynamic_slice_in_dim(q, s0, Q_BLOCK, axis=1).astype(jnp.float32) * scale
        lses, outs = [], []
        for g, (offs, bias, kg_all, vg_all) in enumerate(cfg):
            nk = offs.shape[0]
            kpos = qpos[:, None] + offs[None, :]
            valid = (kpos >= 0) & (kpos < S)
            kidx = jnp.clip(kpos, 0, S - 1).reshape(-1)
            kg = jnp.take(kg_all, kidx, axis=1).reshape(B, Q_BLOCK, nk, HEADS_PER_GROUP, HEAD_DIM)
            vg = jnp.take(vg_all, kidx, axis=1).reshape(B, Q_BLOCK, nk, HEADS_PER_GROUP, HEAD_DIM)
            s = jnp.einsum('bqhd,bqkhd->bhqk', qb[:, :, g], kg.astype(jnp.float32))
            s = s + bias[None, :, None, :]
            s = jnp.where(valid[None, None], s, NEG_INF)
            lse = jax.nn.logsumexp(s, axis=-1)
            p = jnp.exp(s - lse[..., None])
            outs.append(jnp.einsum('bhqk,bqkhd->bqhd', p, vg.astype(jnp.float32)))
            lses.append(lse)
        wts = jax.nn.softmax(jnp.stack(lses, axis=0), axis=0)
        wts = jnp.transpose(wts, (0, 1, 3, 2))[..., None]
        out = jnp.sum(wts * jnp.stack(outs, axis=0), axis=0)
        return out.astype(q.dtype)

    o = lax.map(block, jnp.arange(n_blocks, dtype=jnp.int32))
    o = jnp.transpose(o, (1, 0, 2, 3, 4))
    return o.reshape(B, S, HEADS_PER_GROUP * HEAD_DIM)

def first_inputs(seed: int = 0) -> dict:
    key = jax.random.key(seed)
    ks = jax.random.split(key, 12)
    f32 = jnp.float32
    x = jax.random.normal(ks[0], (BATCH, SEQ, D_MODEL), f32)
    norm_gain = 1.0 + 0.05 * jax.random.normal(ks[1], (DEPTH, D_MODEL), f32)
    w_in = jax.random.normal(ks[2], (DEPTH, D_MODEL, IN_W), f32) * D_MODEL ** -0.5
    b_gate = 0.01 * jax.random.normal(ks[3], (DEPTH, 2, D_MODEL), f32)
    rel_bias = 0.5 * jax.random.normal(ks[4], (NUM_BUCKETS, N_ATT_HEADS), f32)
    w_pool = jax.random.normal(ks[5], (DEPTH, N_POOL_GROUPS, POOL_GROUP_W, POOL_GROUP_W), f32) * POOL_GROUP_W ** -0.5
    pool_scale = 1.0 + 0.1 * jax.random.normal(ks[6], (DEPTH, BRANCH_W), f32)
    w_proj_a = jax.random.normal(ks[7], (DEPTH, BRANCH_W, D_MODEL), f32) * BRANCH_W ** -0.5
    w_proj_b = jax.random.normal(ks[8], (DEPTH, BRANCH_W, D_MODEL), f32) * BRANCH_W ** -0.5
    w_out = jax.random.normal(ks[9], (DEPTH, D_MODEL, D_MODEL), f32) * D_MODEL ** -0.5
    final_gain = 1.0 + 0.05 * jax.random.normal(ks[10], (D_MODEL,), f32)
    return {"x": x, "norm_gain": norm_gain, "w_in": w_in, "b_gate": b_gate,
            "rel_bias": rel_bias, "w_pool": w_pool, "pool_scale": pool_scale,
            "w_proj_a": w_proj_a, "w_proj_b": w_proj_b, "w_out": w_out,
            "final_gain": final_gain}

def first_block(x, norm_gain, w_in, b_gate, rel_bias, w_pool, pool_scale,
              w_proj_a, w_proj_b, w_out, final_gain):
    B, S, D = x.shape
    splits = np.cumsum([BRANCH_W, BRANCH_W, QKV_W, QKV_W, QKV_W, BRANCH_W]).tolist()
    for l in range(DEPTH):
        h = _rmsnorm(x, norm_gain[l])
        z = h @ w_in[l]
        a_in, a_gate, q, k, v, b_gp, g_logits = jnp.split(z, splits, axis=-1)
        y_a = (_multiscale_pool(a_in, w_pool[l], pool_scale[l]) * jax.nn.silu(a_gate)) @ w_proj_a[l]
        shp = (B, S, N_ATT_GROUPS, HEADS_PER_GROUP, HEAD_DIM)
        att = _dilated_attention(q.reshape(shp), k.reshape(shp), v.reshape(shp), rel_bias)
        y_b = (att * jax.nn.silu(b_gp)) @ w_proj_b[l]
        gates = jax.nn.sigmoid(g_logits.reshape(B, S, 2, D) + b_gate[l])
        merged = gates[:, :, 0] * y_a + gates[:, :, 1] * y_b
        x = x + merged @ w_out[l]
    return _rmsnorm(x, final_gain)


DEPTH_2 = 2

N_MIXERS = 2
N_CONV_LAYERS = (DEPTH_2 + N_MIXERS - 1) // N_MIXERS
N_ATTN_LAYERS = DEPTH_2 // N_MIXERS
CONV_WIDTH = 3
N_HEADS = 16
N_KV_HEADS = 4
HEAD_DIM_2 = D_MODEL // N_HEADS
GROUP = N_HEADS // N_KV_HEADS
WINDOW = 128
BLOCK = 128
NEG_INF_2 = -1e30
N_BUCKETS = 32
MAX_DISTANCE_2 = 128
PEER_HEADS = 8
N_KEYS = 128
N_EXPERTS = N_KEYS * N_KEYS
PEER_TOPK = 16
QUERY_DIM = 256
SUB_DIM = QUERY_DIM // 2
PEER_CHUNK = 128


def _rmsnorm_2(x, g):
    xf = x.astype(jnp.float32)
    y = xf * lax.rsqrt(jnp.mean(xf * xf, axis=-1, keepdims=True) + RMS_EPS)
    return (y * g.astype(jnp.float32)).astype(x.dtype)

def _short_conv_mixer(x, w_in, w_conv, w_out):
    gate_b, gate_c, h = jnp.split(x @ w_in, 3, axis=-1)
    y = lax.conv_general_dilated(
        gate_c * h, w_conv[:, None, :].astype(h.dtype),
        window_strides=(1,), padding=((CONV_WIDTH // 2, CONV_WIDTH // 2),),
        dimension_numbers=("NWC", "WIO", "NWC"), feature_group_count=D_MODEL)
    return (gate_b * y) @ w_out

def _t5_bucket_2(rel):
    half = N_BUCKETS // 2
    max_exact = half // 2
    ret = jnp.where(rel > 0, half, 0)
    n = jnp.abs(rel)
    nf = jnp.maximum(n, 1).astype(jnp.float32)
    large = max_exact + (jnp.log(nf / max_exact) / math.log(MAX_DISTANCE_2 / max_exact)
                         * (half - max_exact)).astype(jnp.int32)
    large = jnp.minimum(large, half - 1)
    return ret + jnp.where(n < max_exact, n, large)

def _windowed_gqa(x, w_qkv, sink, w_o, rel_bias):
    bsz, s, _ = x.shape
    nb = s // BLOCK
    qkv = x @ w_qkv
    q = qkv[..., :N_HEADS * HEAD_DIM_2].reshape(bsz, nb, BLOCK, N_KV_HEADS, GROUP, HEAD_DIM_2)
    k = qkv[..., N_HEADS * HEAD_DIM_2:(N_HEADS + N_KV_HEADS) * HEAD_DIM_2].reshape(bsz, s, N_KV_HEADS, HEAD_DIM_2)
    v = qkv[..., (N_HEADS + N_KV_HEADS) * HEAD_DIM_2:].reshape(bsz, s, N_KV_HEADS, HEAD_DIM_2)

    def band(t):
        tp = jnp.pad(t, ((0, 0), (BLOCK, BLOCK), (0, 0), (0, 0)))
        tb = tp.reshape(bsz, nb + 2, BLOCK, N_KV_HEADS, HEAD_DIM_2)
        return jnp.concatenate([tb[:, :-2], tb[:, 1:-1], tb[:, 2:]], axis=2)

    kw, vw = band(k), band(v)
    scores = jnp.einsum("bnqhgd,bnkhd->bnhgqk", q, kw).astype(jnp.float32) / math.sqrt(HEAD_DIM_2)

    qi = jnp.arange(BLOCK)[:, None]
    kj = jnp.arange(3 * BLOCK)[None, :]
    rel = kj - BLOCK - qi
    bias = rel_bias[_t5_bucket_2(rel)].astype(jnp.float32)
    bias = jnp.transpose(bias, (2, 0, 1)).reshape(N_KV_HEADS, GROUP, BLOCK, 3 * BLOCK)
    kpos = jnp.arange(nb)[:, None] * BLOCK - BLOCK + jnp.arange(3 * BLOCK)[None, :]
    valid = (jnp.abs(rel) <= WINDOW)[None] & ((kpos >= 0) & (kpos < s))[:, None, :]
    logits = jnp.where(valid[None, :, None, None], scores + bias, NEG_INF_2)

    sink_logit = jnp.broadcast_to(sink.astype(jnp.float32).reshape(N_KV_HEADS, GROUP, 1, 1),
                                  logits.shape[:-1] + (1,))
    probs = jax.nn.softmax(jnp.concatenate([logits, sink_logit], axis=-1), axis=-1)[..., :-1]
    out = jnp.einsum("bnhgqk,bnkhd->bnqhgd", probs.astype(vw.dtype), vw)
    return out.reshape(bsz, s, N_HEADS * HEAD_DIM_2) @ w_o

def _peer(xn, w_q, subkeys, u_tab, v_tab):
    bsz, s, d = xn.shape
    t = xn.reshape(-1, d)
    n_tok = t.shape[0]
    q = (t @ w_q).reshape(n_tok, PEER_HEADS, 2, SUB_DIM)
    sc = jnp.einsum("thpd,hpnd->thpn", q, subkeys).astype(jnp.float32)
    sv, si = lax.top_k(sc, PEER_TOPK)
    cand = (sv[:, :, 0, :, None] + sv[:, :, 1, None, :]).reshape(n_tok, PEER_HEADS, PEER_TOPK * PEER_TOPK)
    cidx = (si[:, :, 0, :, None] * N_KEYS + si[:, :, 1, None, :]).reshape(n_tok, PEER_HEADS, PEER_TOPK * PEER_TOPK)
    top_v, pos = lax.top_k(cand, PEER_TOPK)
    idx = jnp.take_along_axis(cidx, pos, axis=-1)
    g = jax.nn.softmax(top_v, axis=-1)

    n_chunks = n_tok // PEER_CHUNK
    n_sel = PEER_HEADS * PEER_TOPK

    def expert_block(args):
        xc, ic, gc = args
        u = jnp.take(u_tab, ic, axis=0)
        h = jnp.einsum("cd,ced->ce", xc, u)
        a = gc.astype(xc.dtype) * jax.nn.gelu(h, approximate=False)
        return jnp.einsum("ce,ced->cd", a, jnp.take(v_tab, ic, axis=0))

    out = lax.map(expert_block, (t.reshape(n_chunks, PEER_CHUNK, d),
                                 idx.reshape(n_chunks, PEER_CHUNK, n_sel),
                                 g.reshape(n_chunks, PEER_CHUNK, n_sel)))
    return out.reshape(bsz, s, d)

def second_inputs(seed: int = 0) -> dict:
    key = jax.random.key(seed)
    ks = jax.random.split(key, 20)
    D = D_MODEL
    nrm = lambda k, shape, scale: jax.random.normal(k, shape, jnp.float32) * scale
    qkv_cols = (N_HEADS + 2 * N_KV_HEADS) * HEAD_DIM_2
    return {
        "x": nrm(ks[0], (BATCH, SEQ, D), 1.0),
        "conv_norm_g": 1.0 + nrm(ks[1], (N_CONV_LAYERS, D), 0.02),
        "conv_w_in": nrm(ks[2], (N_CONV_LAYERS, D, 3 * D), D ** -0.5),
        "conv_w": nrm(ks[3], (N_CONV_LAYERS, CONV_WIDTH, D), CONV_WIDTH ** -0.5),
        "conv_w_out": nrm(ks[4], (N_CONV_LAYERS, D, D), D ** -0.5),
        "attn_norm_g": 1.0 + nrm(ks[5], (N_ATTN_LAYERS, D), 0.02),
        "attn_w_qkv": nrm(ks[6], (N_ATTN_LAYERS, D, qkv_cols), D ** -0.5),
        "attn_sink": nrm(ks[7], (N_ATTN_LAYERS, N_HEADS), 0.5),
        "attn_w_o": nrm(ks[8], (N_ATTN_LAYERS, N_HEADS * HEAD_DIM_2, D), (N_HEADS * HEAD_DIM_2) ** -0.5),
        "rel_bias": nrm(ks[9], (N_BUCKETS, N_HEADS), 0.1),
        "ffn_norm_g": 1.0 + nrm(ks[10], (DEPTH_2, D), 0.02),
        "peer_w_q": nrm(ks[11], (DEPTH_2, D, PEER_HEADS * QUERY_DIM), D ** -0.5),
        "peer_subkeys": nrm(ks[12], (DEPTH_2, PEER_HEADS, 2, N_KEYS, SUB_DIM), SUB_DIM ** -0.5),
        "peer_u": nrm(ks[13], (DEPTH_2, N_EXPERTS, D), D ** -0.5),
        "peer_v": nrm(ks[14], (DEPTH_2, N_EXPERTS, D), D ** -0.5),
        "final_norm_g": 1.0 + nrm(ks[15], (D,), 0.02),
    }

def second_block(x, conv_norm_g, conv_w_in, conv_w, conv_w_out, attn_norm_g, attn_w_qkv,
              attn_sink, attn_w_o, rel_bias, ffn_norm_g, peer_w_q, peer_subkeys,
              peer_u, peer_v, final_norm_g):
    for i in range(DEPTH_2):
        j = i // N_MIXERS
        if i % N_MIXERS == 0:
            x = x + _short_conv_mixer(_rmsnorm_2(x, conv_norm_g[j]), conv_w_in[j], conv_w[j], conv_w_out[j])
        else:
            x = x + _windowed_gqa(_rmsnorm_2(x, attn_norm_g[j]), attn_w_qkv[j], attn_sink[j],
                                  attn_w_o[j], rel_bias)
        x = x + _peer(_rmsnorm_2(x, ffn_norm_g[i]), peer_w_q[i], peer_subkeys[i], peer_u[i], peer_v[i])
    return _rmsnorm_2(x, final_norm_g)


def setup_inputs(seed=0):
    out = dict(first_inputs(seed))
    for name, value in second_inputs(seed + 1).items():
        if name != "x":
            out[name + "_2"] = value
    return out


def reference(
    x, norm_gain, w_in, b_gate, rel_bias, w_pool, pool_scale, w_proj_a, w_proj_b, w_out,
    final_gain, conv_norm_g_2, conv_w_in_2, conv_w_2, conv_w_out_2, attn_norm_g_2, attn_w_qkv_2,
    attn_sink_2, attn_w_o_2, rel_bias_2, ffn_norm_g_2, peer_w_q_2, peer_subkeys_2, peer_u_2,
    peer_v_2, final_norm_g_2,
):
    x = first_block(
        x, norm_gain, w_in, b_gate, rel_bias, w_pool, pool_scale, w_proj_a, w_proj_b, w_out,
        final_gain,
    )
    return second_block(
        x, conv_norm_g_2, conv_w_in_2, conv_w_2, conv_w_out_2, attn_norm_g_2, attn_w_qkv_2,
        attn_sink_2, attn_w_o_2, rel_bias_2, ffn_norm_g_2, peer_w_q_2, peer_subkeys_2, peer_u_2,
        peer_v_2, final_norm_g_2,
    )


_drawn_inputs = setup_inputs


def setup_inputs(seed=0):
    import zlib

    import numpy as np

    out = dict(_drawn_inputs(seed))
    spreads = {}
    factors = {'b_gate': 8.0,
     'attn_norm_g_2': 8.0,
     'attn_sink_2': 8.0,
     'rel_bias_2': 8.0,
     'ffn_norm_g_2': 8.0,
     'peer_w_q_2': 3.716,
     'peer_subkeys_2': 3.732,
     'peer_u_2': 4.127,
     'peer_v_2': 3.7,
     'final_norm_g_2': 2.873}
    for name, (base, spread) in spreads.items():
        noise = np.random.default_rng([zlib.crc32(name.encode()), seed]).standard_normal(out[name].shape)
        drawn = base * np.exp(spread * noise) if base else spread * noise
        out[name] = __import__('jax').numpy.asarray(drawn.astype(out[name].dtype))
    for name, factor in factors.items():
        out[name] = (out[name] * factor).astype(out[name].dtype)
    return out
```

```python
from contextlib import ExitStack

import numpy as np

import concourse.bass as bass
from concourse import mybir

F32 = mybir.dt.float32
U32 = mybir.dt.uint32
ALU = mybir.AluOpType
ACT = mybir.ActivationFunctionType
AX_X = mybir.AxisListType.X

P = 128
SEQ = 256
D = 1024
TILES = SEQ // P
KC = D // P
EPS = 1e-6
MASKED = -1e30
ONE = 1
LOWEST = -3e38

BRANCH = 512
A_IN, A_GATE, Q1, K1, V1, B_GATE, G_LOG = 0, 512, 1024, 2560, 4096, 5632, 6144
GROUPS = ((128, 1), (512, 4), (2048, 16))
NG = len(GROUPS)
HEADS1 = 8
HD = 64
POOL_GROUPS = 4
REL = 512
HANKEL = 384

HEADS2 = 16
WINDOW2 = 128
PEER_HEADS = 8
NKEYS = 128
TOPK = 16
EXPERTS = NKEYS * NKEYS
UNITS = PEER_HEADS * TILES
HALF = TOPK // 2

PF_NORM, PF_CONV, PF_ATT, PF_POOL, PF_BG, PF_CW = 0, 8, 16, 24, 28, 44
PF_ALL = 68
C_ID, C_REV, C_INV, C_IOTA = 0, 128, 256, 1280
C_ALL = 1296

FILLS = ([3] * 4 + [1] * 12, [3] * 4 + [1] * 12, [3] * 4 + [1] + [2] * 2 + [1] * 6)


def landed_value(b, use):
    return 16 * sum(FILLS[b][:use + 1])


def buckets(rel, far):
    n = np.abs(rel)
    nf = np.maximum(n, 1).astype(np.float32)
    large = 8 + (np.log(nf / np.float32(8)) / np.float32(np.log(far / 8)) * np.float32(8)).astype(np.int32)
    return np.where(rel > 0, 16, 0) + np.where(n < 8, n, np.minimum(large, 15))


def bucket_table():
    rel = np.arange(REL) - (SEQ - 1)
    inside = np.abs(rel) < SEQ
    rows = []
    for window, dil in GROUPS:
        rows.append(np.where(inside & (rel % dil == 0) & (np.abs(rel) <= window // 2), buckets(rel, 1024), 32))
    rows.append(np.where(inside & (np.abs(rel) <= WINDOW2), buckets(rel, 128), 32))
    return (np.arange(33)[:, None] == np.concatenate(rows)[None, :]).astype(np.float32)


def constants():
    c = np.zeros((P, C_ALL), np.float32)
    c[:, C_ID:C_ID + P] = np.eye(P)
    c[:, C_REV:C_REV + P] = np.eye(P)[::-1]
    pos = np.arange(SEQ)
    for g in range(POOL_GROUPS):
        half = 1 << g
        count = np.minimum(pos + half - 1, SEQ - 1) - np.maximum(pos - half, 0) + 1
        c[:, C_INV + g * SEQ:C_INV + (g + 1) * SEQ] = np.float32(1) / count.astype(np.float32)
    c[:, C_IOTA:C_IOTA + TOPK] = np.arange(TOPK)
    return c


def build(nc, A, out):
    with ExitStack() as ctx:
        def sb(name, shape, dt=F32):
            return ctx.enter_context(nc.sbuf_tensor(name, shape, dt))

        def sem(name):
            return ctx.enter_context(nc.semaphore(name))

        bias_rows1 = nc.dram_tensor("bias_rows1", [HEADS1, NG, REL], F32)
        bias_rows2 = nc.dram_tensor("bias_rows2", [HEADS2, REL], F32)

        ps = [ctx.enter_context(nc.psum_tensor(f"ps{i}", [P, 1024], F32)) for i in range(4)]
        psA, psB, psC, psD = ps
        wbuf = sb("wbuf", [P, 3, KC, 512])
        x = sb("x", [P, TILES, D])
        xn = sb("xn", [P, TILES, D])
        hT = sb("hT", [P, KC, SEQ])
        gain_row = sb("gain_row", [P, D])
        pf = sb("pf", [P, PF_ALL])
        const = sb("const", [P, C_ALL])
        rb = sb("rb", [P, 24 + HEADS2])
        sinks = sb("sinks", [P, HEADS2])
        sumsq = sb("sumsq", [P, TILES])
        meansq = sb("meansq", [P, TILES])
        root = sb("root", [P, TILES])
        rinv = sb("rinv", [P, TILES])
        small = sb("small", [P, 64])
        arena = sb("arena", [P, 30720])

        ident = const[:, C_ID:C_ID + P]
        reverse = const[:, C_REV:C_REV + P]
        inv_count = const[:, C_INV:C_INV + 4 * SEQ].rearrange("p (g t) -> p g t", g=4)
        iota16 = const[:, C_IOTA:C_IOTA + TOPK]

        def at(first, *shape):
            n = int(np.prod(shape))
            v = arena[:, first:first + n]
            if len(shape) == 2:
                v = v.rearrange("p (a b) -> p a b", a=shape[0])
            elif len(shape) == 3:
                v = v.rearrange("p (a b c) -> p a b c", a=shape[0], b=shape[1])
            return v

        hank1 = at(0, 24, HANKEL)
        qz = at(9216, 2, NG, SEQ)
        kT = at(10752, NG, SEQ)
        v1 = at(11520, TILES, NG * P)
        prob1 = at(12288, 2, 768)
        probT1 = at(13824, 2, 6, P)
        att1 = at(15360, TILES, BRANCH)
        bucket = at(16384, 4 * REL)
        row1 = at(18432, NG, REL)
        row2 = at(19968, REL)
        PAD = 8
        uT = at(16384, 4, SEQ + 2 * PAD)
        win2 = at(17472, 4, SEQ + 2 * PAD)
        win4 = at(18560, 4, SEQ + 2 * PAD)
        win8 = at(19648, 4, SEQ + 2 * PAD)
        pooled = at(20736, 4, SEQ)
        gate_a = at(21760, 4 * SEQ)
        gate_b = at(22784, 4 * SEQ)
        sig_a = at(23808, 4 * SEQ)
        sig_b = at(24832, 4 * SEQ)
        yaT = at(25856, 4, SEQ)
        ybT = at(26880, 4, SEQ)
        prod_a = at(0, 4 * SEQ)
        prod_b = at(1024, 4 * SEQ)
        merged = at(2048, KC, SEQ)
        wpool = at(4096, 4, P)
        gate_c = at(4608, 4 * SEQ)
        cu = at(5632, 4, SEQ + 2)
        cacc = at(6664, 4, SEQ)
        cT = at(7688, KC, SEQ)
        uring = at(0, HALF, D)
        vring = at(8192, HALF, D)
        pqT = at(8192, 16, SEQ)
        scores = at(16384, TILES, 16 * NKEYS)
        diag = at(20480, 2, HALF, P)
        work = at(22528, 2, 2, NKEYS)
        cand = at(23040, TOPK * TOPK)
        onehot = at(23296, 2, TOPK, TOPK)
        top_v = at(23808, 2, TOPK)
        top_i = at(23840, 2, TOPK).bitcast(U32)
        sel_v = at(23872, TOPK)
        sel_p = at(23888, TOPK).bitcast(U32)
        sel_i = at(23904, TOPK).bitcast(U32)
        sel_j = at(23920, TOPK).bitcast(U32)
        key_ij = at(23936, 2, TOPK)
        expert = at(23968, 2, TOPK).bitcast(U32)
        gate_e = at(24000, TOPK)
        gate = at(24016, 2, TOPK)
        dot = at(24048, 2, TOPK)
        act_e = at(24080, 2, TOPK)
        coef = at(24112, 2, TOPK)
        subk = at(28672, 16, NKEYS)
        hank2 = at(0, HEADS2, HANKEL)
        qz2 = at(6144, 8, SEQ)
        kT2 = at(8192, 2 * SEQ)
        v2 = at(8704, TILES, 256)
        prob2 = at(9216, 4, 264)
        probT2 = at(10272, 4, 2, P)
        att2 = at(11296, TILES, D)
        zeros = at(28544, P)

        x_loaded = sem("x_loaded")
        const_loaded = sem("const_loaded")
        param_loaded = sem("param_loaded")
        sinks_loaded = sem("sinks_loaded")
        rb_cleared = sem("rb_cleared")
        rb_loaded = sem("rb_loaded")
        pads_zero = sem("pads_zero")
        zeros_ready = sem("zeros_ready")
        rows_done = sem("rows_done")
        rows_copied = sem("rows_copied")
        rows_stored = sem("rows_stored")
        hank1_loaded = sem("hank1_loaded")
        hank2_loaded = sem("hank2_loaded")
        gain_loaded = sem("gain_loaded")
        subk_loaded = sem("subk_loaded")
        wpool_loaded = sem("wpool_loaded")
        w_landed = [sem(f"w_landed{b}") for b in range(3)]
        chunk_done = [sem(f"chunk_done{b}") for b in range(3)]
        sumsq_done = sem("sumsq_done")
        meansq_done = sem("meansq_done")
        root_done = sem("root_done")
        xn_done = sem("xn_done")
        turned = sem("turned")
        turned_act = sem("turned_act")
        turned_dve = sem("turned_dve")
        dve_step = sem("dve_step")
        act_step = sem("act_step")
        q1_copied = sem("q1_copied")
        k1_copied = sem("k1_copied")
        v1_copied = sem("v1_copied")
        sc1_done = sem("sc1_done")
        max1_done = sem("max1_done")
        exp1_done = sem("exp1_done")
        probT1_done = sem("probT1_done")
        probT1_copied = sem("probT1_copied")
        av1_done = sem("av1_done")
        att1_done = sem("att1_done")
        sig_done = sem("sig_done")
        gates_done = sem("gates_done")
        pooled_done = sem("pooled_done")
        mixed_done = sem("mixed_done")
        att1_turned = sem("att1_turned")
        ya_done = sem("ya_done")
        yb_done = sem("yb_done")
        merge_sig = sem("merge_sig")
        merged_done = sem("merged_done")
        x_added = sem("x_added")
        gc_copied = sem("gc_copied")
        conv_done = sem("conv_done")
        kv2_copied = sem("kv2_copied")
        v2_copied = sem("v2_copied")
        q2_copied = sem("q2_copied")
        sc2_done = sem("sc2_done")
        max2_done = sem("max2_done")
        exp2_done = sem("exp2_done")
        probT2_done = sem("probT2_done")
        probT2_copied = sem("probT2_copied")
        av2_done = sem("av2_done")
        att2_done = sem("att2_done")
        pq_act = sem("pq_act")
        pq_dve = sem("pq_dve")
        keys_done = sem("keys_done")
        scores_act = sem("scores_act")
        scores_dve = sem("scores_dve")
        staged = sem("staged")
        topk_done = sem("topk_done")
        gate_exp = sem("gate_exp")
        expert_ready = sem("expert_ready")
        u_landed = [sem(f"u_landed{e}") for e in range(HALF)]
        v_landed = [sem(f"v_landed{e}") for e in range(HALF)]
        dots_done = sem("dots_done")
        gelu_done = sem("gelu_done")
        coef_done = sem("coef_done")
        diag_done = sem("diag_done")
        v_used = sem("v_used")
        out_stored = sem("out_stored")
        dve_waited = sem("dve_waited")
        pool_waited = sem("pool_waited")

        counts_from_one = [*chunk_done, sc1_done, exp1_done, probT1_done, probT1_copied, av1_done,
                           att1_done, sc2_done, exp2_done, probT2_done, probT2_copied,
                           av2_done, att2_done, dots_done, v_used]

        w_in = A["w_in"][0].rearrange("(k p) c -> p k c", p=P)

        def cols(w, first, n):
            return w.rearrange("(k p) c -> p k c", p=P)[:, :, first:first + n]

        block = ctx.enter_context(nc.Block())

        @block.sync
        def _(sp):
            sp.dma_start(x[:], A["x"][0].rearrange("(t p) d -> p t d", p=P)).then_inc(x_loaded, 16)
            sp.dma_start(const[:], A["const"]).then_inc(const_loaded, 16)
            sp.dma_start(bucket[0:33], A["bucket"]).then_inc(const_loaded, 16)
            sp.dma_start(pf[:], A["pf"]).then_inc(param_loaded, 16)
            sp.dma_start(gain_row[:], A["final_gain"].partition_broadcast(P)).then_inc(gain_loaded, 16)

            with sp.Fori(0, HEADS1 // 2) as i:
                for b, first in enumerate((Q1, K1, V1)):
                    sp.wait_ge(chunk_done[b], ONE + i)
                    for g in range(NG):
                        sp.dma_start(wbuf[:, b, :, g * P:(g + 1) * P],
                                     w_in[:, :, bass.ds(i * P + (first + g * 512), P)]).then_inc(w_landed[b], 16)

            def load(b, use, src):
                sp.wait_ge(chunk_done[b], ONE + use)
                sp.dma_start(wbuf[:, b], src).then_inc(w_landed[b], 16)

            load(0, 4, w_in[:, :, A_IN:A_IN + 512])
            load(1, 4, w_in[:, :, A_GATE:A_GATE + 512])
            load(2, 4, w_in[:, :, B_GATE:B_GATE + 512])
            for j in range(2):
                load(0, 5 + j, w_in[:, :, G_LOG + j * 512:G_LOG + (j + 1) * 512])
                load(1, 5 + j, w_in[:, :, G_LOG + D + j * 512:G_LOG + D + (j + 1) * 512])
                sp.wait_ge(chunk_done[2], ONE + 5 + j)
                sp.dma_start(wbuf[:, 2, 0:4], cols(A["w_proj_a"][0], j * 512, 512)).then_inc(w_landed[2], 16)
                sp.dma_start(wbuf[:, 2, 4:8], cols(A["w_proj_b"][0], j * 512, 512)).then_inc(w_landed[2], 16)
            load(0, 7, cols(A["w_out"][0], 0, 512))
            load(1, 7, cols(A["w_out"][0], 512, 512))
            for j in range(2):
                load(0, 8 + j, cols(A["conv_w_in_2"][0], j * 512, 512))
                load(1, 8 + j, cols(A["conv_w_in_2"][0], D + j * 512, 512))
                load(2, 7 + j, cols(A["conv_w_in_2"][0], 2 * D + j * 512, 512))
            load(0, 10, cols(A["conv_w_out_2"][0], 0, 512))
            load(1, 10, cols(A["conv_w_out_2"][0], 512, 512))

            sp.wait_ge(xn_done, 4)
            sp.dma_start(subk, A["subk"][0].rearrange("p (c n) -> p c n", c=16)).then_inc(subk_loaded, 16)
            sp.dma_start(gain_row[:], A["ffn_norm_g_2"][0].partition_broadcast(P)).then_inc(gain_loaded, 16)
            for c, (b, use) in enumerate(((2, 9), (0, 11), (1, 11), (2, 10))):
                load(b, use, cols(A["peer_w_q_2"][0], c * 512, 512))
            load(0, 12, cols(A["attn_w_qkv_2"][0], D, 512))
            sp.wait_ge(xn_done, 8)
            sp.dma_start(gain_row[:], A["ffn_norm_g_2"][1].partition_broadcast(P)).then_inc(gain_loaded, 16)
            sp.wait_ge(keys_done, 4)
            sp.dma_start(subk, A["subk"][1].rearrange("p (c n) -> p c n", c=16)).then_inc(subk_loaded, 16)
            qkv = A["attn_w_qkv_2"][0].rearrange("(k p) c -> p k c", p=P)
            with sp.Fori(0, 2) as c:
                sp.wait_ge(chunk_done[1], ONE + c + 12)
                sp.dma_start(wbuf[:, 1], qkv[:, :, bass.ds(c * 512, 512)]).then_inc(w_landed[1], 16)
            load(0, 13, cols(A["attn_w_o_2"][0], 0, 512))
            load(2, 11, cols(A["attn_w_o_2"][0], 512, 512))
            for c, (b, use) in enumerate(((0, 14), (1, 14), (2, 12), (0, 15))):
                load(b, use, cols(A["peer_w_q_2"][1], c * 512, 512))
            sp.wait_ge(xn_done, 12)
            sp.dma_start(gain_row[:], A["final_norm_g_2"].partition_broadcast(P)).then_inc(gain_loaded, 16)
            for t in range(TILES):
                sp.wait_ge(xn_done, 13 + t)
                sp.dma_start(out[t * P:(t + 1) * P], xn[:, t]).then_inc(out_stored, 16)
            sp.wait_ge(out_stored, 16 * TILES)

        @block.gpsimd
        def _(pool):
            for s in counts_from_one:
                pool.sem_inc(s, ONE)
            nc.gpsimd.memset(rb[:], MASKED).then_inc(rb_cleared, 1)
            pool.wait_ge(rb_cleared, 1)
            pool.dma_start(rb[0:32, 0:24], A["rel_bias"]).then_inc(rb_loaded, 16)
            pool.dma_start(rb[0:32, 24:40], A["rel_bias_2"]).then_inc(rb_loaded, 16)
            pool.dma_start(sinks[:], A["attn_sink_2"][0].partition_broadcast(P)).then_inc(sinks_loaded, 16)
            nc.gpsimd.memset(qz[:], 0.0).then_inc(pads_zero, 1)
            pool.wait_ge(rows_copied, 2)
            pool.dma_start(bias_rows1.ap(), row1[0:HEADS1]).then_inc(rows_stored, 16)
            pool.dma_start(bias_rows2.ap(), row2[0:HEADS2]).then_inc(rows_stored, 16)
            pool.wait_ge(rows_stored, 32)
            pool.dma_start(hank1, bass.AP(bias_rows1, 0, [[1, P], [REL, HEADS1 * NG], [1, HANKEL]])).then_inc(hank1_loaded, 16)
            nc.gpsimd.memset(uT[:], 0.0).then_inc(pads_zero, 1)
            pool.wait_ge(att1_done, ONE + 16)
            pool.dma_start(wpool, A["w_pool"][0].rearrange("g c d -> c g d")).then_inc(wpool_loaded, 16)
            nc.gpsimd.memset(cu[:], 0.0).then_inc(pads_zero, 1)

            def gathers(layer):
                def half(unit, t, b):
                    n = unit * 2 + b
                    pool.wait_ge(dots_done, ONE + n)
                    pool.sem_inc(pool_waited, 1)
                    for e in range(HALF):
                        idx = expert[:, t, b * HALF + e:b * HALF + e + 1]
                        pool.indirect_dma_start(uring[:, e], None, A["peer_u_2"],
                                                bass.IndirectOffsetOnAxis(ap=idx, axis=0)).then_inc(u_landed[e], 16)
                    pool.wait_ge(v_used, ONE + n)
                    pool.sem_inc(pool_waited, 1)
                    for e in range(HALF):
                        idx = expert[:, t, b * HALF + e:b * HALF + e + 1]
                        pool.indirect_dma_start(vring[:, e], None, A["peer_v_2"],
                                                bass.IndirectOffsetOnAxis(ap=idx, axis=0)).then_inc(v_landed[e], 16)

                with pool.Fori(0, PEER_HEADS) as h:
                    for t in range(TILES):
                        unit = h * TILES + (UNITS * layer + t)
                        pool.wait_ge(expert_ready, unit + 1)
                        for b in range(2):
                            half(unit, t, b)

            gathers(0)
            pool.wait_ge(x_added, 6)
            pool.dma_start(hank2, bass.AP(bias_rows2, 0, [[1, P], [REL, HEADS2], [1, HANKEL]])).then_inc(hank2_loaded, 16)
            nc.gpsimd.memset(qz2[:], 0.0).then_inc(pads_zero, 1)
            gathers(1)

        @block.scalar
        def _(act):
            def norm(k, junk_free=None):
                for t in range(TILES):
                    nc.scalar.activation(xn[:, t], x[:, t], ACT.Square, accum_out=sumsq[:, t:t + 1]).then_inc(sumsq_done, 1)
                act.wait_ge(meansq_done, k + 1)
                nc.scalar.activation(root[:], meansq[:], ACT.Sqrt).then_inc(root_done, 1)

            def turned_out(n, gain):
                for bank in (0, 2):
                    act.wait_ge(turned, 4 * n + bank + 1)
                    for c in (2 * bank, 2 * bank + 1):
                        src = ps[bank // 2][:, (c % 4) * SEQ:(c % 4 + 1) * SEQ]
                        if gain is None:
                            last = nc.scalar.activation(hT[:, c], src, ACT.Copy)
                        else:
                            last = nc.scalar.activation(hT[:, c], src, ACT.Copy, scale=pf[:, gain + c:gain + c + 1])
                    last.then_inc(turned_act, 1)

            act.wait_ge(x_loaded, 16)
            norm(0)
            act.wait_ge(rows_done, 1)
            nc.scalar.activation(row1[0:HEADS1, 0:2], psC[0:HEADS1, :].rearrange("p (g m) -> p g m", g=2), ACT.Copy)
            nc.scalar.activation(row1[0:HEADS1, 2], psD[0:HEADS1, 0:512], ACT.Copy).then_inc(rows_copied, 1)
            nc.scalar.activation(row2[0:HEADS2], psD[0:HEADS2, 512:1024], ACT.Copy).then_inc(rows_copied, 1)
            act.wait_ge(param_loaded, 16)
            turned_out(0, PF_NORM)

            act.wait_ge(pads_zero, 1)
            with act.Fori(0, HEADS1 // 2) as i:
                act.wait_ge(chunk_done[0], ONE + i + 1)
                act.wait_ge(sc1_done, ONE + i * 4)
                for a in range(2):
                    r = slice(64 * a, 64 * a + 64)
                    last = nc.scalar.activation(qz[r, a], psA[r, 0:768].rearrange("p (g t) -> p g t", g=NG), ACT.Copy,
                                                scale=HD ** -0.5)
                last.then_inc(q1_copied, 1)

                def exp(u):
                    act.wait_ge(max1_done, i * 4 + u + 1)
                    act.wait_ge(probT1_done, ONE + i * 4 + max(u - 1, 0))
                    nc.scalar.activation(prob1[:, u % 2], ps[2 + u % 2][:, 0:768], ACT.Exp, bias=small[:, u:u + 1],
                                         accum_out=small[:, 4 + u:5 + u]).then_inc(exp1_done, 1)

                exp(0)
                exp(1)
                act.wait_ge(chunk_done[2], ONE + i + 1)
                act.wait_ge(av1_done, ONE + i * 4)
                nc.scalar.activation(v1[:], psA[:].rearrange("p (t c) -> p t c", t=TILES)[:, :, 0:NG * P], ACT.Copy)\
                    .then_inc(v1_copied, 1)
                exp(2)
                exp(3)

            for n, (b, src, dst) in enumerate(((1, psB, sig_a), (2, psC, sig_b))):
                act.wait_ge(chunk_done[b], ONE + 5)
                nc.scalar.activation(dst, src[:], ACT.Sigmoid).then_inc(sig_done, 1)

            for j in range(2):
                act.wait_ge(merged_done, j) if j else act.wait_ge(gates_done, 2)
                for n, (b, src, dst) in enumerate(((0, psA, sig_a), (1, psB, sig_b))):
                    act.wait_ge(chunk_done[b], ONE + 6 + j)
                    for m in range(4):
                        bias = pf[:, PF_BG + 8 * n + 4 * j + m:PF_BG + 8 * n + 4 * j + m + 1]
                        last = nc.scalar.activation(dst[:, m * SEQ:(m + 1) * SEQ], src[:, m * SEQ:(m + 1) * SEQ],
                                                    ACT.Sigmoid, bias=bias)
                    last.then_inc(merge_sig, 1)

            act.wait_ge(x_added, 2)
            norm(1)
            act.wait_ge(xn_done, 4)
            norm(2)
            turned_out(1, PF_CONV)

            for j in range(2):
                act.wait_ge(chunk_done[1], ONE + 9 + j)
                if j:
                    act.wait_ge(conv_done, 1)
                nc.scalar.activation(gate_c, psB[:], ACT.Copy).then_inc(gc_copied, 1)

            def peer(layer):
                n = 3 + 2 * layer
                norm(n)
                turned_out(2 + 3 * layer, None)
                fills = (((2, 10), (0, 12), (1, 12), (2, 11)), ((0, 15), (1, 15), (2, 13), (0, 16)))[layer]
                for c in (0, 2):
                    b, use = fills[c]
                    act.wait_ge(chunk_done[b], ONE + use)
                    nc.scalar.activation(pqT[:, 4 * c:4 * c + 4], ps[c][:].rearrange("p (m t) -> p m t", m=4), ACT.Copy)\
                        .then_inc(pq_act, 1)
                for t in range(TILES):
                    act.wait_ge(keys_done, 4 * layer + 2 * t + 1)
                    nc.scalar.activation(scores[:, t, 0:1024], ps[2 * t][:], ACT.Copy).then_inc(scores_act, 1)
                act.wait_ge(scores_dve, 2 * layer + 2)
                act.wait_ge(scores_act, 2 * layer + 2)

                def stage(h, t):
                    nc.scalar.activation(work[:, t], scores[:, t, bass.ds(h * 256, 256)].rearrange("p (a n) -> p a n", a=2),
                                         ACT.Copy).then_inc(staged, 1)

                def softmax_exp(unit, t):
                    act.wait_ge(topk_done, unit + 1)
                    nc.scalar.activation(gate_e, sel_v, ACT.Exp, bias=small[:, 8:9], accum_out=small[:, 9:10]).then_inc(gate_exp, 1)

                def mix(unit, t, b):
                    n = unit * 2 + b
                    e0 = b * HALF
                    act.wait_ge(dots_done, ONE + n + 1)
                    nc.scalar.activation(act_e[:, t, e0:e0 + HALF], dot[:, t, e0:e0 + HALF], ACT.Gelu).then_inc(gelu_done, 1)
                    act.wait_ge(coef_done, n + 1)
                    act.wait_ge(v_used, ONE + unit * 2)
                    for e in range(HALF):
                        nc.scalar.activation(diag[:, b, e], ident, ACT.Copy, scale=coef[:, t, e0 + e:e0 + e + 1])\
                            .then_inc(diag_done, 1)

                base = UNITS * layer

                def pair(h, last):
                    for t in range(TILES):
                        unit = h * TILES + (base + t)
                        if t == 0:
                            stage(h, 1)
                        elif not last:
                            stage(h + 1, 0)
                        mix(unit, t, 0)
                        mix(unit, t, 1)
                        if t == 0 or not last:
                            softmax_exp(unit + 1, 1 - t)

                stage(0, 0)
                softmax_exp(base, 0)
                with act.Fori(0, PEER_HEADS - 1) as h:
                    pair(h, False)
                pair(PEER_HEADS - 1, True)

            act.wait_ge(x_added, 4)
            peer(0)

            act.wait_ge(x_added, 6)
            norm(4)
            turned_out(3, PF_ATT)
            act.wait_ge(chunk_done[0], ONE + 13)
            nc.scalar.activation(kT2, psC[:, 0:512], ACT.Copy).then_inc(kv2_copied, 1)
            act.wait_ge(pads_zero, 4)
            with act.Fori(0, 2) as c:
                act.wait_ge(chunk_done[1], ONE + c + 13)
                act.wait_ge(sc2_done, ONE + c * 16)
                for i in range(8):
                    to, of = slice(64 * (i // 4), 64 * (i // 4) + 64), slice(64 * (i % 2), 64 * (i % 2) + 64)
                    last = nc.scalar.activation(qz2[to, i], psA[of, (i // 2) * SEQ:(i // 2 + 1) * SEQ], ACT.Copy,
                                                scale=HD ** -0.5)
                last.then_inc(q2_copied, 1)
                for u in range(16):
                    act.wait_ge(max2_done, c * 16 + u + 1)
                    act.wait_ge(probT2_done, ONE + c * 16 + max(u - 3, 0))
                    nc.scalar.activation(prob2[:, u % 4, 0:257], ps[2 + u // 2 % 2][:, (u % 2) * 512:(u % 2) * 512 + 257], ACT.Exp,
                                         bias=small[:, 16 + u:17 + u], accum_out=small[:, 32 + u:33 + u]).then_inc(exp2_done, 1)
            turned_out(4, None)

            act.wait_ge(x_added, 8)
            peer(1)
            act.wait_ge(x_added, 10)
            norm(6)

        @block.tensor
        def _(pe):
            mm = nc.tensor.matmul

            def turn(n, src):
                for bank in range(4):
                    for c in (2 * bank, 2 * bank + 1):
                        for t in range(TILES):
                            last = nc.tensor.transpose(ps[bank // 2][:, (c % 4) * SEQ + t * P:(c % 4) * SEQ + (t + 1) * P],
                                                       src[:, t, c * P:(c + 1) * P], ident)
                    last.then_inc(turned, 1)

            def turned_in(n):
                pe.wait_ge(turned_act, 2 * n + 2)
                pe.wait_ge(turned_dve, 2 * n + 2)

            def columns(dst, b, use, src=hT, k0=0, k1=KC, count=True):
                pe.wait_ge(w_landed[b], landed_value(b, use))
                for m in range(4):
                    for k in range(k0, k1):
                        last = mm(dst[:, m * SEQ:(m + 1) * SEQ], wbuf[:, b, k, m * P:(m + 1) * P], src[:, k - k0],
                                  start=(k == k0), stop=(k == k1 - 1))
                if count:
                    last.then_inc(chunk_done[b], 1)

            def rows(dst, b, use, src):
                pe.wait_ge(w_landed[b], landed_value(b, use))
                for t in range(TILES):
                    for k in range(KC):
                        last = mm(dst[:, t * 512:(t + 1) * 512], src[:, k, t * P:(t + 1) * P], wbuf[:, b, k],
                                  start=(k == 0), stop=(k == KC - 1))
                last.then_inc(chunk_done[b], 1)

            pe.wait_ge(const_loaded, 32)
            pe.wait_ge(rb_loaded, 32)
            for n in range(4):
                heads = HEADS1 if n < NG else HEADS2
                last = mm(ps[2 + n // 2][0:heads, (n % 2) * 512:(n % 2 + 1) * 512], rb[0:33, 8 * n:8 * n + heads],
                          bucket[0:33, n * REL:(n + 1) * REL], start=True, stop=True)
            last.then_inc(rows_done, 1)

            pe.wait_ge(xn_done, 2)
            turn(0, xn)
            turned_in(0)

            pe.wait_ge(rows_copied, 2)
            pe.wait_ge(hank1_loaded, 16)
            with pe.Fori(0, HEADS1 // 2) as i:
                def project(dst, b):
                    pe.wait_ge(w_landed[b], i * 48 + 48)
                    for g in range(NG):
                        for k in range(KC):
                            last = mm(dst[:, g * SEQ:(g + 1) * SEQ], wbuf[:, b, k, g * P:(g + 1) * P], hT[:, k],
                                      start=(k == 0), stop=(k == KC - 1))
                    last.then_inc(chunk_done[b], 1)

                def score(u):
                    a, t, dst = u // 2, u % 2, ps[2 + u % 2]
                    pe.wait_ge(exp1_done, ONE + i * 4 + max(u - 1, 0))
                    for g in range(NG):
                        mm(dst[:, g * SEQ:(g + 1) * SEQ], qz[:, a, g, t * P:(t + 1) * P], kT[:, g], start=True, stop=False)
                        last = mm(dst[:, g * SEQ:(g + 1) * SEQ], reverse,
                                  arena[:, bass.ds(i * (6 * HANKEL) + ((a * NG + g) * HANKEL + P * (1 - t)), SEQ)],
                                  start=False, stop=True)
                    last.then_inc(sc1_done, 1)

                def turn_probs(u):
                    pe.wait_ge(exp1_done, ONE + i * 4 + u + 1)
                    pe.wait_ge(probT1_copied, ONE + i * 4 + u)
                    for m in range(6):
                        last = nc.tensor.transpose(psB[:, m * P:(m + 1) * P], prob1[:, u % 2, m * P:(m + 1) * P], ident)
                    last.then_inc(probT1_done, 1)

                def times_v(u):
                    a = u // 2
                    pe.wait_ge(probT1_copied, ONE + i * 4 + u + 1)
                    pe.wait_ge(att1_done, ONE + i * 4 + max(u - 1, 0))
                    for m in range(6):
                        g, kt = m // 2, m % 2
                        last = mm(psA[:, (u % 2) * 512:(u % 2) * 512 + HD], probT1[:, u % 2, m],
                                  v1[:, kt, g * P + a * HD:g * P + a * HD + HD], start=(m == 0), stop=(m == 5))
                    last.then_inc(av1_done, 1)

                pe.wait_ge(att1_done, ONE + i * 4)
                project(psA, 0)
                pe.wait_ge(probT1_copied, ONE + i * 4)
                project(psB, 1)
                pe.wait_ge(q1_copied, i + 1)
                pe.wait_ge(k1_copied, i + 1)
                score(0)
                score(1)
                pe.wait_ge(w_landed[2], i * 48 + 48)
                for t in range(TILES):
                    for k in range(KC):
                        last = mm(psA[:, t * 512:t * 512 + NG * P], hT[:, k, t * P:(t + 1) * P], wbuf[:, 2, k, 0:NG * P],
                                  start=(k == 0), stop=(k == KC - 1))
                last.then_inc(chunk_done[2], 1)
                turn_probs(0)
                score(2)
                turn_probs(1)
                pe.wait_ge(v1_copied, i + 1)
                times_v(0)
                score(3)
                turn_probs(2)
                times_v(1)
                turn_probs(3)
                times_v(2)
                times_v(3)

            pe.wait_ge(att1_done, ONE + 16)
            columns(psA, 0, 4)
            pe.wait_ge(probT1_copied, ONE + 16)
            columns(psB, 1, 4)
            pe.wait_ge(exp1_done, ONE + 16)
            columns(psC, 2, 4)
            for m in range(4):
                for t in range(TILES):
                    last = nc.tensor.transpose(psD[:, m * SEQ + t * P:m * SEQ + (t + 1) * P], att1[:, t, m * P:(m + 1) * P], ident)
            last.then_inc(att1_turned, 1)
            pe.wait_ge(pooled_done, 1)
            pe.wait_ge(wpool_loaded, 16)
            for g in range(POOL_GROUPS):
                last = mm(psA[:, g * SEQ:(g + 1) * SEQ], wpool[:, g], pooled[:, g], start=True, stop=True)
            last.then_inc(mixed_done, 1)
            for j in range(2):
                if j == 0:
                    pe.wait_ge(ya_done, 1)
                    pe.wait_ge(gates_done, 2)
                else:
                    pe.wait_ge(merge_sig, 2)
                columns(psA, 0, 5 + j)
                columns(psB, 1, 5 + j)
                if j == 0:
                    pe.wait_ge(yb_done, 1)
                else:
                    pe.wait_ge(merged_done, 1)
                columns(psC, 2, 5 + j, src=yaT, k0=0, k1=4, count=False)
                columns(psD, 2, 5 + j, src=ybT, k0=4, k1=8)
            pe.wait_ge(merge_sig, 4)
            pe.wait_ge(merged_done, 2)
            rows(psA, 0, 7, merged)
            rows(psB, 1, 7, merged)

            pe.wait_ge(x_added, 2)
            pe.wait_ge(xn_done, 6)
            turn(1, xn)
            turned_in(1)
            for j in range(2):
                if j:
                    pe.wait_ge(conv_done, 1)
                columns(psA, 0, 8 + j)
                columns(psB, 1, 8 + j)
                columns(psC, 2, 7 + j)
            pe.wait_ge(conv_done, 2)
            rows(psA, 0, 10, cT)
            rows(psB, 1, 10, cT)

            def peer(layer):
                n = 3 + 2 * layer
                pe.wait_ge(x_added, (4, 8)[layer])
                pe.wait_ge(xn_done, (8, 12)[layer])
                turn(2 + 3 * layer, xn)
                turned_in(2 + 3 * layer)
                fills = (((2, 9), (0, 11), (1, 11), (2, 10)), ((0, 14), (1, 14), (2, 12), (0, 15)))[layer]
                for c, (b, use) in enumerate(fills):
                    columns(ps[c], b, use)
                pe.wait_ge(pq_act, 2 * layer + 2)
                pe.wait_ge(pq_dve, 2 * layer + 2)
                pe.wait_ge(subk_loaded, 16 * (layer + 1))
                for t in range(TILES):
                    for s in range(2):
                        for m in range(8):
                            last = mm(ps[2 * t + s][:, m * NKEYS:(m + 1) * NKEYS], pqT[:, 8 * s + m, t * P:(t + 1) * P],
                                      subk[:, 8 * s + m], start=True, stop=True)
                        last.then_inc(keys_done, 1)
                pe.wait_ge(scores_act, 2 * layer + 2)
                pe.wait_ge(scores_dve, 2 * layer + 2)
                pe.wait_ge(zeros_ready, 1)
                for t in range(TILES):
                    for s in range(2):
                        mm(ps[t][:, s * 512:(s + 1) * 512], zeros, xn[:, 0, 0:512], start=True, stop=False,
                           skip_group_check=True)
                with pe.Fori(0, PEER_HEADS) as h:
                    for t in range(TILES):
                        unit = h * TILES + (UNITS * layer + t)
                        for b in range(2):
                            n = unit * 2 + b
                            for e in range(HALF):
                                pe.wait_ge(v_landed[e], n * 16 + 16)
                                pe.wait_ge(diag_done, n * HALF + (e + 1))
                                for s in range(2):
                                    last = mm(ps[t][:, s * 512:(s + 1) * 512], diag[:, b, e], vring[:, e, s * 512:(s + 1) * 512],
                                              start=False, stop=False, skip_group_check=True)
                            last.then_inc(v_used, 1)

            peer(0)

            pe.wait_ge(x_added, 6)
            pe.wait_ge(xn_done, 10)
            turn(3, xn)
            turned_in(3)
            pe.wait_ge(w_landed[0], landed_value(0, 12))
            for m in range(2):
                for k in range(KC):
                    mm(psC[:, m * SEQ:(m + 1) * SEQ], wbuf[:, 0, k, m * P:(m + 1) * P], hT[:, k], start=(k == 0), stop=(k == KC - 1))
            for t in range(TILES):
                for k in range(KC):
                    last = mm(psC[:, 512 + t * 256:512 + (t + 1) * 256], hT[:, k, t * P:(t + 1) * P], wbuf[:, 0, k, 256:512],
                              start=(k == 0), stop=(k == KC - 1))
            last.then_inc(chunk_done[0], 1)
            pe.wait_ge(kv2_copied, 1)
            pe.wait_ge(v2_copied, 1)
            pe.wait_ge(hank2_loaded, 16)
            pe.wait_ge(sinks_loaded, 16)
            with pe.Fori(0, 2) as c:
                pe.wait_ge(w_landed[1], c * 16 + landed_value(1, 12))
                pe.wait_ge(att2_done, ONE + c * 16)
                for m in range(4):
                    for k in range(KC):
                        last = mm(psA[:, m * SEQ:(m + 1) * SEQ], wbuf[:, 1, k, m * P:(m + 1) * P], hT[:, k],
                                  start=(k == 0), stop=(k == KC - 1))
                last.then_inc(chunk_done[1], 1)
                pe.wait_ge(q2_copied, c + 1)

                def score(u):
                    i, t = u // 2, u % 2
                    dst = ps[2 + u // 2 % 2][:, (u % 2) * 512:(u % 2) * 512 + 257]
                    pe.wait_ge(exp2_done, ONE + c * 16 + max(u - 3, 0))
                    mm(dst[:, 256:257], reverse, sinks[:, bass.ds(c * 8 + i, 1)], start=True, stop=True)
                    mm(dst[:, 0:256], qz2[:, i, t * P:(t + 1) * P], kT2[:, bass.ds(c * SEQ, SEQ)], start=True, stop=False)
                    mm(dst[:, 0:256], reverse, arena[:, bass.ds(c * (8 * HANKEL) + (i * HANKEL + P * (1 - t)), SEQ)],
                       start=False, stop=True).then_inc(sc2_done, 1)

                def turn_probs(u):
                    pe.wait_ge(exp2_done, ONE + c * 16 + u + 1)
                    pe.wait_ge(probT2_copied, ONE + c * 16 + max(u - 1, 0))
                    for kt in range(2):
                        last = nc.tensor.transpose(psB[:, (u % 2) * 512 + kt * P:(u % 2) * 512 + (kt + 1) * P],
                                                   prob2[:, u % 4, kt * P:(kt + 1) * P], ident)
                    last.then_inc(probT2_done, 1)

                def times_v(u):
                    i = u // 2
                    pe.wait_ge(probT2_copied, ONE + c * 16 + u + 1)
                    pe.wait_ge(att2_done, ONE + c * 16 + max(u - 1, 0))
                    for kt in range(2):
                        last = mm(psA[:, (u % 2) * 512:(u % 2) * 512 + HD], probT2[:, u % 4, kt],
                                  v2[:, kt, bass.ds(c * P + (i // 4) * HD, HD)], start=(kt == 0), stop=(kt == 1))
                    last.then_inc(av2_done, 1)

                for s in range(16 + 3):
                    if s < 16:
                        score(s)
                    if 0 <= s - 2 < 16:
                        turn_probs(s - 2)
                    if 0 <= s - 3 < 16:
                        times_v(s - 3)
            pe.wait_ge(att2_done, ONE + 32)
            turn(4, att2)
            turned_in(4)
            rows(psA, 0, 13, hT)
            rows(psB, 2, 11, hT)
            peer(1)

        @block.vector
        def _(dve):
            class Chain:
                first, n = 0, 0

                def link(self, ins):
                    self.n += 1
                    ins.then_inc(dve_step, 1)
                    dve.wait_ge(dve_step, self.first + self.n)

                def loop(self, i, per):
                    self.before, self.first, self.n, self.per = self.first + self.n, i * per + (self.first + self.n), 0, per

                def end(self, times):
                    assert self.n == self.per, self.n
                    self.first, self.n = self.before + times * self.per, 0

            chain = Chain()
            link = chain.link

            def norm(k):
                dve.wait_ge(sumsq_done, 2 * k + 2)
                nc.vector.tensor_scalar(meansq[:], sumsq[:], 1.0 / D, EPS, ALU.mult, ALU.add).then_inc(meansq_done, 1)
                dve.wait_ge(meansq_done, k + 1)
                dve.wait_ge(root_done, k + 1)
                link(nc.vector.reciprocal(root[:], root[:]))
                link(nc.vector.tensor_tensor(rinv[:], root[:], root[:], ALU.mult))
                link(nc.vector.tensor_tensor(rinv[:], rinv[:], meansq[:], ALU.mult))
                link(nc.vector.tensor_scalar(rinv[:], rinv[:], -0.5, 1.5, ALU.mult, ALU.add))
                link(nc.vector.tensor_tensor(rinv[:], rinv[:], root[:], ALU.mult))

            def plain(k):
                norm(k)
                for t in range(TILES):
                    nc.vector.tensor_scalar(xn[:, t], x[:, t], rinv[:, t:t + 1], None, ALU.mult).then_inc(xn_done, 1)

            def with_gain(k, gains, dst):
                norm(k)
                dve.wait_ge(gain_loaded, 16 * gains)
                for t in range(TILES):
                    nc.vector.scalar_tensor_tensor(out=dst[:, t], in0=x[:, t], scalar=rinv[:, t:t + 1], in1=gain_row[:],
                                                   op0=ALU.mult, op1=ALU.mult).then_inc(xn_done, 1)

            def turned_out(n, gain):
                for bank in (1, 3):
                    dve.wait_ge(turned, 4 * n + bank + 1)
                    for c in (2 * bank, 2 * bank + 1):
                        src = ps[bank // 2][:, (c % 4) * SEQ:(c % 4 + 1) * SEQ]
                        if gain is None:
                            last = nc.vector.tensor_copy(hT[:, c], src)
                        else:
                            last = nc.vector.tensor_scalar(hT[:, c], src, pf[:, gain + c:gain + c + 1], None, ALU.mult)
                    last.then_inc(turned_dve, 1)

            def residual(added, waits):
                for j, (s, value) in enumerate(waits):
                    dve.wait_ge(s, value)
                    dst = x[:, :, j * 512:(j + 1) * 512]
                    nc.vector.tensor_tensor(dst, ps[j][:].rearrange("p (t c) -> p t c", t=TILES), dst, ALU.add).then_inc(x_added, 1)

            nc.vector.memset(zeros, 0.0).then_inc(zeros_ready, 1)
            plain(0)
            dve.wait_ge(param_loaded, 16)
            turned_out(0, PF_NORM)

            with dve.Fori(0, HEADS1 // 2) as i:
                chain.loop(i, 4)
                dve.wait_ge(chunk_done[1], ONE + i + 1)
                dve.wait_ge(sc1_done, ONE + i * 4)
                nc.vector.tensor_copy(kT[:], psB[:, 0:768].rearrange("p (g t) -> p g t", g=NG)).then_inc(k1_copied, 1)

                def row_max(u):
                    dve.wait_ge(sc1_done, ONE + i * 4 + u + 1)
                    dve.wait_ge(exp1_done, ONE + i * 4 + max(u - 1, 0))
                    nc.vector.tensor_reduce(small[:, u:u + 1], ps[2 + u % 2][:, 0:768], AX_X, ALU.max, negate=True)\
                        .then_inc(max1_done, 1)

                def copy_probs(u):
                    dve.wait_ge(probT1_done, ONE + i * 4 + u + 1)
                    dve.wait_ge(av1_done, ONE + i * 4 + max(u - 1, 0))
                    nc.vector.tensor_copy(probT1[:, u % 2], psB[:, 0:768].rearrange("p (m t) -> p m t", m=6))\
                        .then_inc(probT1_copied, 1)

                def output(u):
                    a, t = u // 2, u % 2
                    link(nc.vector.reciprocal(small[:, 10 + u:11 + u], small[:, 4 + u:5 + u]))
                    dve.wait_ge(av1_done, ONE + i * 4 + u + 1)
                    nc.vector.tensor_scalar(att1[:, t, bass.ds(i * P + a * HD, HD)], psA[:, (u % 2) * 512:(u % 2) * 512 + HD],
                                            small[:, 10 + u:11 + u], None, ALU.mult).then_inc(att1_done, 1)

                row_max(0)
                row_max(1)
                copy_probs(0)
                row_max(2)
                copy_probs(1)
                output(0)
                row_max(3)
                copy_probs(2)
                output(1)
                copy_probs(3)
                output(2)
                output(3)
            chain.end(HEADS1 // 2)

            dve.wait_ge(pads_zero, 2)
            dve.wait_ge(chunk_done[0], ONE + 5)
            link(nc.vector.tensor_copy(uT[:, :, PAD:PAD + SEQ], psA[:].rearrange("p (g t) -> p g t", g=4)))

            def window(dst, src, g, lo, hi, shift):
                left = 1 if shift == 0 else shift
                link(nc.vector.tensor_tensor(dst[:, g:4, PAD + lo:PAD + hi], src[:, g:4, PAD + lo - left:PAD + hi - left],
                                             src[:, g:4, PAD + lo + shift:PAD + hi + shift], ALU.add))

            window(win2, uT, 0, -7, SEQ + 7, 0)
            window(win4, win2, 1, -6, SEQ + 6, 1)
            window(win8, win4, 2, -4, SEQ + 4, 2)
            window(win2, win8, 3, 0, SEQ, 4)
            sums = (win2, win4, win8, win2)
            for g in range(4):
                last = nc.vector.tensor_tensor(pooled[:, g], sums[g][:, g, PAD:PAD + SEQ], inv_count[:, g], ALU.mult)
            link(last)
            nc.vector.tensor_tensor(pooled[:], pooled[:], uT[:, :, PAD:PAD + SEQ], ALU.subtract).then_inc(pooled_done, 1)

            dve.wait_ge(sig_done, 1)
            nc.vector.tensor_tensor(gate_a, psB[:], sig_a, ALU.mult).then_inc(gates_done, 1)
            dve.wait_ge(sig_done, 2)
            nc.vector.tensor_tensor(gate_b, psC[:], sig_b, ALU.mult).then_inc(gates_done, 1)
            dve.wait_ge(gates_done, 2)
            dve.wait_ge(att1_turned, 1)
            nc.vector.tensor_tensor(ybT[:].rearrange("p m t -> p (m t)"), psD[:], gate_b, ALU.mult).then_inc(yb_done, 1)
            dve.wait_ge(mixed_done, 1)
            for g in range(POOL_GROUPS):
                last = nc.vector.scalar_tensor_tensor(out=yaT[:, g], in0=psA[:, g * SEQ:(g + 1) * SEQ],
                                                      scalar=pf[:, PF_POOL + g:PF_POOL + g + 1],
                                                      in1=gate_a[:, g * SEQ:(g + 1) * SEQ], op0=ALU.mult, op1=ALU.mult)
            last.then_inc(ya_done, 1)
            for j in range(2):
                dve.wait_ge(merge_sig, 2 * j + 2)
                dve.wait_ge(chunk_done[2], ONE + 6 + j)
                nc.vector.tensor_tensor(prod_a, psC[:], sig_a, ALU.mult)
                link(nc.vector.tensor_tensor(prod_b, psD[:], sig_b, ALU.mult))
                nc.vector.tensor_tensor(merged[:, 4 * j:4 * j + 4].rearrange("p m t -> p (m t)"), prod_a, prod_b, ALU.add)\
                    .then_inc(merged_done, 1)
            dve.wait_ge(merged_done, 2)
            residual(2, ((chunk_done[0], ONE + 8), (chunk_done[1], ONE + 8)))
            dve.wait_ge(x_added, 2)
            with_gain(1, 1, x)
            dve.wait_ge(xn_done, 4)
            plain(2)
            turned_out(1, PF_CONV)

            dve.wait_ge(pads_zero, 3)
            for j in range(2):
                dve.wait_ge(gc_copied, j + 1)
                dve.wait_ge(chunk_done[2], ONE + 8 + j)
                link(nc.vector.tensor_tensor(cu[:, :, 1:1 + SEQ], psC[:].rearrange("p (m t) -> p m t", m=4),
                                             gate_c.rearrange("p (m t) -> p m t", m=4), ALU.mult))
                for tap in range(3):
                    for m in range(4):
                        w = pf[:, PF_CW + tap * KC + 4 * j + m:PF_CW + tap * KC + 4 * j + m + 1]
                        if tap == 0:
                            last = nc.vector.tensor_scalar(cacc[:, m], cu[:, m, 0:SEQ], w, None, ALU.mult)
                        else:
                            last = nc.vector.scalar_tensor_tensor(out=cacc[:, m], in0=cu[:, m, tap:tap + SEQ], scalar=w,
                                                                  in1=cacc[:, m], op0=ALU.mult, op1=ALU.add)
                    link(last)
                dve.wait_ge(chunk_done[0], ONE + 9 + j)
                nc.vector.tensor_tensor(cT[:, 4 * j:4 * j + 4], psA[:].rearrange("p (m t) -> p m t", m=4), cacc[:], ALU.mult)\
                    .then_inc(conv_done, 1)
                dve.wait_ge(conv_done, j + 1)
            residual(4, ((chunk_done[0], ONE + 11), (chunk_done[1], ONE + 11)))

            def peer(layer):
                dve.wait_ge(x_added, (4, 8)[layer])
                with_gain(3 + 2 * layer, 2 + layer, xn)
                turned_out(2 + 3 * layer, None)
                fills = (((2, 10), (0, 12), (1, 12), (2, 11)), ((0, 15), (1, 15), (2, 13), (0, 16)))[layer]
                for c in (1, 3):
                    b, use = fills[c]
                    dve.wait_ge(chunk_done[b], ONE + use)
                    nc.vector.tensor_copy(pqT[:, 4 * c:4 * c + 4], ps[c][:].rearrange("p (m t) -> p m t", m=4)).then_inc(pq_dve, 1)
                for t in range(TILES):
                    dve.wait_ge(keys_done, 4 * layer + 2 * t + 2)
                    nc.vector.tensor_copy(scores[:, t, 1024:2048], ps[2 * t + 1][:]).then_inc(scores_dve, 1)

                def apart():
                    dve.sem_inc(dve_waited, 1)

                def linked(ins):
                    link(ins)
                    apart()

                def top16(values, indices, src, n):
                    for p in range(n):
                        last = nc.vector.max(values(p, 0), src(p))
                    linked(last)
                    for p in range(n):
                        last = nc.vector.max_index(indices(p, 0), values(p, 0), src(p))
                    linked(last)
                    for p in range(n):
                        last = nc.vector.match_replace(src(p), values(p, 0), src(p), LOWEST)
                    linked(last)
                    for p in range(n):
                        last = nc.vector.max(values(p, 1), src(p))
                    linked(last)
                    for p in range(n):
                        last = nc.vector.max_index(indices(p, 1), values(p, 1), src(p))
                    linked(last)

                def topk(unit, t):
                    dve.wait_ge(staged, unit + 1)
                    apart()
                    top16(lambda p, r: top_v[:, p, 8 * r:8 * r + 8], lambda p, r: top_i[:, p, 8 * r:8 * r + 8],
                          lambda p: work[:, t, p], 2)
                    grid = cand.rearrange("p (a b) -> p a b", a=TOPK)
                    linked(nc.vector.tensor_tensor(grid, top_v[:, 0].unsqueeze(2).to_broadcast([P, TOPK, TOPK]),
                                                 top_v[:, 1].unsqueeze(1).to_broadcast([P, TOPK, TOPK]), ALU.add))
                    top16(lambda p, r: sel_v[:, 8 * r:8 * r + 8], lambda p, r: sel_p[:, 8 * r:8 * r + 8], lambda p: cand, 1)
                    nc.vector.tensor_scalar(small[:, 8:9], sel_v[:, 0:1], -1.0, None, ALU.mult).then_inc(topk_done, 1)
                    nc.vector.tensor_scalar(sel_i, sel_p, 4, None, ALU.logical_shift_right)
                    link(nc.vector.tensor_scalar(sel_j, sel_p, 15, None, ALU.bitwise_and))
                    for p, sel in enumerate((sel_i, sel_j)):
                        last = nc.vector.tensor_tensor(onehot[:, p], sel.unsqueeze(2).to_broadcast([P, TOPK, TOPK]),
                                                       iota16.unsqueeze(1).to_broadcast([P, TOPK, TOPK]), ALU.is_equal)
                    link(last)
                    for p in range(2):
                        last = nc.vector.tensor_tensor(onehot[:, p], onehot[:, p],
                                                       top_i[:, p].unsqueeze(1).to_broadcast([P, TOPK, TOPK]), ALU.mult)
                    link(last)
                    link(nc.vector.tensor_reduce(key_ij[:], onehot[:], AX_X, ALU.add))
                    link(nc.vector.tensor_scalar(key_ij[:, 0], key_ij[:, 0], float(NKEYS), float(EXPERTS * layer), ALU.mult, ALU.add))
                    dve.wait_ge(v_used, ONE + 2 * unit - 2 if not isinstance(unit, int) else max(2 * unit - 2, 0))
                    nc.vector.tensor_tensor(expert[:, t], key_ij[:, 0], key_ij[:, 1], ALU.add).then_inc(expert_ready, 1)
                    dve.wait_ge(gate_exp, unit + 1)
                    link(nc.vector.reciprocal(small[:, 14:15], small[:, 9:10]))
                    link(nc.vector.tensor_scalar(gate[:, t], gate_e, small[:, 14:15], None, ALU.mult))

                STEPS = 18

                def dots(unit, t, b):
                    n = unit * 2 + b
                    for e in range(HALF):
                        dve.wait_ge(u_landed[e], n * 16 + 16)
                        last = nc.vector.tensor_tensor_reduce(out=uring[:, e], in0=xn[:, t], in1=uring[:, e], scale=1.0,
                                                              scalar=0.0, op0=ALU.mult, op1=ALU.add,
                                                              accum_out=dot[:, t, b * HALF + e:b * HALF + e + 1])
                    last.then_inc(dots_done, 1)

                def coefs(unit, t, b):
                    n = unit * 2 + b
                    dve.wait_ge(gelu_done, n + 1)
                    e = slice(b * HALF, (b + 1) * HALF)
                    nc.vector.tensor_tensor(coef[:, t, e], act_e[:, t, e], gate[:, t, e], ALU.mult).then_inc(coef_done, 1)

                base = UNITS * layer

                def pair(h, last):
                    for t in range(TILES):
                        unit = h * TILES + (base + t)
                        for b in range(2):
                            dots(unit, t, b)
                            coefs(unit, t, b)
                        if t == 0 or not last:
                            topk(unit + 1, 1 - t)

                topk(base, 0)
                with dve.Fori(0, PEER_HEADS - 1) as h:
                    chain.loop(h, 2 * STEPS)
                    pair(h, False)
                chain.end(PEER_HEADS - 1)
                pair(PEER_HEADS - 1, True)
                for t in range(TILES):
                    dve.wait_ge(v_used, ONE + 2 * UNITS * (layer + 1))
                    nc.vector.tensor_tensor(x[:, t], ps[t][:], x[:, t], ALU.add).then_inc(x_added, 1)

            peer(0)

            dve.wait_ge(x_added, 6)
            plain(4)
            turned_out(3, PF_ATT)
            dve.wait_ge(chunk_done[0], ONE + 13)
            nc.vector.tensor_copy(v2[:], psC[:, 512:1024].rearrange("p (t c) -> p t c", t=TILES)).then_inc(v2_copied, 1)
            with dve.Fori(0, 2) as c:
                chain.loop(c, 16)

                def row_max(u):
                    dve.wait_ge(sc2_done, ONE + c * 16 + u + 1)
                    nc.vector.tensor_reduce(small[:, 16 + u:17 + u], ps[2 + u // 2 % 2][:, (u % 2) * 512:(u % 2) * 512 + 257],
                                            AX_X, ALU.max, negate=True).then_inc(max2_done, 1)

                def copy_probs(u):
                    dve.wait_ge(probT2_done, ONE + c * 16 + u + 1)
                    dve.wait_ge(av2_done, ONE + c * 16 + max(u - 3, 0))
                    nc.vector.tensor_copy(probT2[:, u % 4], psB[:, (u % 2) * 512:(u % 2) * 512 + 256].rearrange(
                        "p (m t) -> p m t", m=2)).then_inc(probT2_copied, 1)

                def output(u):
                    i, t = u // 2, u % 2
                    link(nc.vector.reciprocal(small[:, 48 + u % 2:49 + u % 2], small[:, 32 + u:33 + u]))
                    dve.wait_ge(av2_done, ONE + c * 16 + u + 1)
                    nc.vector.tensor_scalar(att2[:, t, bass.ds(c * 512 + i * HD, HD)], psA[:, (u % 2) * 512:(u % 2) * 512 + HD],
                                            small[:, 48 + u % 2:49 + u % 2], None, ALU.mult).then_inc(att2_done, 1)

                for s in range(16 + 3):
                    if s < 16:
                        row_max(s)
                    if 0 <= s - 2 < 16:
                        copy_probs(s - 2)
                    if 0 <= s - 3 < 16:
                        output(s - 3)
            chain.end(2)
            turned_out(4, None)
            residual(8, ((chunk_done[0], ONE + 14), (chunk_done[2], ONE + 12)))
            peer(1)
            dve.wait_ge(x_added, 10)
            with_gain(6, 4, xn)


def kernel(**inputs):
    import concourse.bacc as bacc
    from concourse.bass_utils import run_bass_kernel_spmd

    def raw(name):
        return np.ascontiguousarray(inputs[name])

    def feature_columns(v):
        return np.ascontiguousarray(np.reshape(v, (-1, P)).T)

    arrays = {n: raw(n) for n in ("x", "w_in", "rel_bias", "w_pool", "w_proj_a", "w_proj_b", "w_out", "final_gain",
                                  "conv_w_in_2", "conv_w_out_2", "attn_w_qkv_2", "attn_sink_2", "attn_w_o_2",
                                  "rel_bias_2", "ffn_norm_g_2", "peer_w_q_2", "final_norm_g_2")}
    for n in ("peer_u_2", "peer_v_2"):
        arrays[n] = raw(n).reshape(2 * EXPERTS, D)
    arrays["subk"] = np.ascontiguousarray(raw("peer_subkeys_2").transpose(0, 4, 1, 2, 3).reshape(2, P, 16 * NKEYS))
    arrays["pf"] = np.concatenate([feature_columns(raw(n)) for n in (
        "norm_gain", "conv_norm_g_2", "attn_norm_g_2", "pool_scale", "b_gate", "conv_w_2")], axis=1)
    arrays["const"] = constants()
    arrays["bucket"] = bucket_table()

    nc = bacc.Bacc("TRN2", target_bir_lowering=False, num_devices=1)
    aps = {n: nc.dram_tensor(f"in_{n}", a.shape, mybir.dt.from_np(a.dtype), kind="ExternalInput").ap()
           for n, a in arrays.items()}
    out = nc.dram_tensor("out", (SEQ, D), F32, kind="ExternalOutput").ap()
    build(nc, aps, out)
    r = run_bass_kernel_spmd(nc, [{f"in_{n}": a for n, a in arrays.items()}], core_ids=[0])
    return r.results[0]["out"].reshape(1, SEQ, D)
```

```python
from contextlib import ExitStack

import numpy as np

import concourse.bass as bass
from concourse import mybir

F32 = mybir.dt.float32
U32 = mybir.dt.uint32
ALU = mybir.AluOpType
ACT = mybir.ActivationFunctionType
AX_X = mybir.AxisListType.X

P = 128
SEQ = 256
D = 1024
TILES = SEQ // P
KC = D // P
EPS = 1e-6
MASKED = -1e30
ONE = 1
LOWEST = -3e38

BRANCH = 512
A_IN, A_GATE, Q1, K1, V1, B_GATE, G_LOG = 0, 512, 1024, 2560, 4096, 5632, 6144
GROUPS = ((128, 1), (512, 4), (2048, 16))
NG = len(GROUPS)
HEADS1 = 8
HD = 64
POOL_GROUPS = 4
REL = 512
HANKEL = 384

HEADS2 = 16
WINDOW2 = 128
PEER_HEADS = 8
NKEYS = 128
TOPK = 16
EXPERTS = NKEYS * NKEYS
UNITS = PEER_HEADS * TILES
HALF = TOPK // 2

PF_NORM, PF_CONV, PF_ATT, PF_POOL, PF_BG, PF_CW = 0, 8, 16, 24, 28, 44
PF_ALL = 68
C_ID, C_REV, C_INV, C_IOTA = 0, 128, 256, 1280
C_ALL = 1296

FILLS = ([3] * 4 + [1] * 14, [3] * 4 + [1] * 9, [3] * 4 + [1] + [2] * 2 + [1] * 6)
QUERY_FILLS = (((2, 9), (0, 11)), ((2, 12), (0, 15)))


def landed_value(b, use):
    return 16 * sum(FILLS[b][:use + 1])


def buckets(rel, far):
    n = np.abs(rel)
    nf = np.maximum(n, 1).astype(np.float32)
    large = 8 + (np.log(nf / np.float32(8)) / np.float32(np.log(far / 8)) * np.float32(8)).astype(np.int32)
    return np.where(rel > 0, 16, 0) + np.where(n < 8, n, np.minimum(large, 15))


def bucket_table():
    rel = np.arange(REL) - (SEQ - 1)
    inside = np.abs(rel) < SEQ
    rows = []
    for window, dil in GROUPS:
        rows.append(np.where(inside & (rel % dil == 0) & (np.abs(rel) <= window // 2), buckets(rel, 1024), 32))
    rows.append(np.where(inside & (np.abs(rel) <= WINDOW2), buckets(rel, 128), 32))
    return (np.arange(33)[:, None] == np.concatenate(rows)[None, :]).astype(np.float32)


def constants():
    c = np.zeros((P, C_ALL), np.float32)
    c[:, C_ID:C_ID + P] = np.eye(P)
    c[:, C_REV:C_REV + P] = np.eye(P)[::-1]
    pos = np.arange(SEQ)
    for g in range(POOL_GROUPS):
        half = 1 << g
        count = np.minimum(pos + half - 1, SEQ - 1) - np.maximum(pos - half, 0) + 1
        c[:, C_INV + g * SEQ:C_INV + (g + 1) * SEQ] = np.float32(1) / count.astype(np.float32)
    c[:, C_IOTA:C_IOTA + TOPK] = np.arange(TOPK)
    return c


def build(nc, A, out):
    with ExitStack() as ctx:
        def sb(name, shape, dt=F32):
            return ctx.enter_context(nc.sbuf_tensor(name, shape, dt))

        def sem(name):
            return ctx.enter_context(nc.semaphore(name))

        bias_rows1 = nc.dram_tensor("bias_rows1", [HEADS1, NG, REL], F32)
        bias_rows2 = nc.dram_tensor("bias_rows2", [HEADS2, REL], F32)

        ps = [ctx.enter_context(nc.psum_tensor(f"ps{i}", [P, 1024], F32)) for i in range(4)]
        psA, psB, psC, psD = ps
        wbuf = sb("wbuf", [P, 3, KC, 512])
        x = sb("x", [P, TILES, D])
        xn = sb("xn", [P, TILES, D])
        hT = sb("hT", [P, KC, SEQ])
        gain_row = sb("gain_row", [P, D])
        pf = sb("pf", [P, PF_ALL])
        const = sb("const", [P, C_ALL])
        rb = sb("rb", [P, 24 + HEADS2])
        sinks = sb("sinks", [P, HEADS2])
        sumsq = sb("sumsq", [P, TILES])
        meansq = sb("meansq", [P, TILES])
        root = sb("root", [P, TILES])
        rinv = sb("rinv", [P, TILES])
        small = sb("small", [P, 64])
        arena = sb("arena", [P, 30720])

        ident = const[:, C_ID:C_ID + P]
        reverse = const[:, C_REV:C_REV + P]
        inv_count = const[:, C_INV:C_INV + 4 * SEQ].rearrange("p (g t) -> p g t", g=4)
        iota16 = const[:, C_IOTA:C_IOTA + TOPK]

        def at(first, *shape):
            n = int(np.prod(shape))
            v = arena[:, first:first + n]
            if len(shape) == 2:
                v = v.rearrange("p (a b) -> p a b", a=shape[0])
            elif len(shape) == 3:
                v = v.rearrange("p (a b c) -> p a b c", a=shape[0], b=shape[1])
            return v

        hank1 = at(0, 24, HANKEL)
        qz = at(9216, 2, NG, SEQ)
        kT = at(10752, NG, SEQ)
        v1 = at(11520, TILES, NG * P)
        prob1 = at(12288, 2, 768)
        probT1 = at(13824, 2, 6, P)
        att1 = at(15360, TILES, BRANCH)
        bucket = at(16384, 4 * REL)
        row1 = at(18432, NG, REL)
        row2 = at(19968, REL)
        PAD = 8
        uT = at(16384, 4, SEQ + 2 * PAD)
        win2 = at(17472, 4, SEQ + 2 * PAD)
        win4 = at(18560, 4, SEQ + 2 * PAD)
        win8 = at(19648, 4, SEQ + 2 * PAD)
        pooled = at(20736, 4, SEQ)
        gate_a = at(21760, 4 * SEQ)
        gate_b = at(22784, 4 * SEQ)
        sig_a = at(23808, 4 * SEQ)
        sig_b = at(24832, 4 * SEQ)
        yaT = at(25856, 4, SEQ)
        ybT = at(26880, 4, SEQ)
        prod_a = at(0, 4 * SEQ)
        prod_b = at(1024, 4 * SEQ)
        merged = at(2048, KC, SEQ)
        wpool = at(4096, 4, P)
        gate_c = at(4608, 4 * SEQ)
        cu = at(5632, 4, SEQ + 2)
        cacc = at(6664, 4, SEQ)
        cT = at(7688, KC, SEQ)
        uring = at(0, HALF, D)
        vring = at(8192, HALF, D)
        pqT = at(16384, 4, SEQ)
        scores = at(17408, TILES, 4, NKEYS)
        diag = at(20480, 2, HALF, P)
        cand = at(23040, TOPK * TOPK)
        onehot = at(23296, 2, TOPK, TOPK)
        top_v = at(23808, 2, TOPK)
        top_i = at(23840, 2, TOPK).bitcast(U32)
        sel_v = at(23872, TOPK)
        sel_p = at(23888, TOPK).bitcast(U32)
        sel_i = at(23904, TOPK).bitcast(U32)
        sel_j = at(23920, TOPK).bitcast(U32)
        key_ij = at(23936, 2, TOPK)
        expert = at(23968, 2, TOPK).bitcast(U32)
        gate_e = at(24000, TOPK)
        gate = at(24016, 2, TOPK)
        dot = at(24048, 2, TOPK)
        act_e = at(24080, 2, TOPK)
        coef = at(24112, 2, TOPK)
        SUBK = 28672
        subk = at(SUBK, 16, NKEYS)
        hank2 = at(0, HEADS2, HANKEL)
        qz2 = at(6144, 8, SEQ)
        kT2 = at(8192, 2 * SEQ)
        v2 = at(8704, TILES, 256)
        prob2 = at(9216, 4, 264)
        probT2 = at(10272, 4, 2, P)
        att2 = at(11296, TILES, D)
        zeros = at(28544, P)

        x_loaded = sem("x_loaded")
        const_loaded = sem("const_loaded")
        param_loaded = sem("param_loaded")
        sinks_loaded = sem("sinks_loaded")
        rb_cleared = sem("rb_cleared")
        rb_loaded = sem("rb_loaded")
        pads_zero = sem("pads_zero")
        zeros_ready = sem("zeros_ready")
        rows_done = sem("rows_done")
        rows_copied = sem("rows_copied")
        rows_stored = sem("rows_stored")
        hank1_loaded = sem("hank1_loaded")
        hank2_loaded = sem("hank2_loaded")
        gain_loaded = sem("gain_loaded")
        subk_loaded = sem("subk_loaded")
        wpool_loaded = sem("wpool_loaded")
        w_landed = [sem(f"w_landed{b}") for b in range(3)]
        chunk_done = [sem(f"chunk_done{b}") for b in range(3)]
        sumsq_done = sem("sumsq_done")
        meansq_done = sem("meansq_done")
        root_done = sem("root_done")
        xn_done = sem("xn_done")
        turned = sem("turned")
        turned_act = sem("turned_act")
        turned_dve = sem("turned_dve")
        dve_step = sem("dve_step")
        act_step = sem("act_step")
        q1_copied = sem("q1_copied")
        k1_copied = sem("k1_copied")
        v1_copied = sem("v1_copied")
        sc1_done = sem("sc1_done")
        max1_done = sem("max1_done")
        exp1_done = sem("exp1_done")
        probT1_done = sem("probT1_done")
        probT1_copied = sem("probT1_copied")
        av1_done = sem("av1_done")
        att1_done = sem("att1_done")
        sig_done = sem("sig_done")
        gates_done = sem("gates_done")
        pooled_done = sem("pooled_done")
        mixed_done = sem("mixed_done")
        att1_turned = sem("att1_turned")
        ya_done = sem("ya_done")
        yb_done = sem("yb_done")
        merge_sig = sem("merge_sig")
        merged_done = sem("merged_done")
        x_added = sem("x_added")
        gc_copied = sem("gc_copied")
        conv_done = sem("conv_done")
        kv2_copied = sem("kv2_copied")
        v2_copied = sem("v2_copied")
        q2_copied = sem("q2_copied")
        sc2_done = sem("sc2_done")
        max2_done = sem("max2_done")
        exp2_done = sem("exp2_done")
        probT2_done = sem("probT2_done")
        probT2_copied = sem("probT2_copied")
        av2_done = sem("av2_done")
        att2_done = sem("att2_done")
        pq_copied = sem("pq_copied")
        keys_done = sem("keys_done")
        scores_ready = sem("scores_ready")
        topk_done = sem("topk_done")
        gate_exp = sem("gate_exp")
        expert_ready = sem("expert_ready")
        u_landed = [sem(f"u_landed{e}") for e in range(HALF)]
        v_landed = [sem(f"v_landed{e}") for e in range(HALF)]
        dots_done = sem("dots_done")
        gelu_done = sem("gelu_done")
        coef_done = sem("coef_done")
        diag_done = sem("diag_done")
        v_used = sem("v_used")
        out_stored = sem("out_stored")
        dve_waited = sem("dve_waited")
        pool_waited = sem("pool_waited")

        counts_from_one = [*chunk_done, sc1_done, exp1_done, probT1_done, probT1_copied, av1_done,
                           att1_done, sc2_done, exp2_done, probT2_done, probT2_copied,
                           av2_done, att2_done, dots_done, v_used, keys_done, topk_done]

        w_in = A["w_in"][0].rearrange("(k p) c -> p k c", p=P)

        def cols(w, first, n):
            return w.rearrange("(k p) c -> p k c", p=P)[:, :, first:first + n]

        block = ctx.enter_context(nc.Block())

        @block.sync
        def _(sp):
            sp.dma_start(x[:], A["x"][0].rearrange("(t p) d -> p t d", p=P)).then_inc(x_loaded, 16)
            sp.dma_start(const[:], A["const"]).then_inc(const_loaded, 16)
            sp.dma_start(bucket[0:33], A["bucket"]).then_inc(const_loaded, 16)
            sp.dma_start(pf[:], A["pf"]).then_inc(param_loaded, 16)
            sp.dma_start(gain_row[:], A["final_gain"].partition_broadcast(P)).then_inc(gain_loaded, 16)

            with sp.Fori(0, HEADS1 // 2) as i:
                for b, first in enumerate((Q1, K1, V1)):
                    sp.wait_ge(chunk_done[b], ONE + i)
                    for g in range(NG):
                        sp.dma_start(wbuf[:, b, :, g * P:(g + 1) * P],
                                     w_in[:, :, bass.ds(i * P + (first + g * 512), P)]).then_inc(w_landed[b], 16)

            def load(b, use, src):
                sp.wait_ge(chunk_done[b], ONE + use)
                sp.dma_start(wbuf[:, b], src).then_inc(w_landed[b], 16)

            load(0, 4, w_in[:, :, A_IN:A_IN + 512])
            load(1, 4, w_in[:, :, A_GATE:A_GATE + 512])
            load(2, 4, w_in[:, :, B_GATE:B_GATE + 512])
            for j in range(2):
                load(0, 5 + j, w_in[:, :, G_LOG + j * 512:G_LOG + (j + 1) * 512])
                load(1, 5 + j, w_in[:, :, G_LOG + D + j * 512:G_LOG + D + (j + 1) * 512])
                sp.wait_ge(chunk_done[2], ONE + 5 + j)
                sp.dma_start(wbuf[:, 2, 0:4], cols(A["w_proj_a"][0], j * 512, 512)).then_inc(w_landed[2], 16)
                sp.dma_start(wbuf[:, 2, 4:8], cols(A["w_proj_b"][0], j * 512, 512)).then_inc(w_landed[2], 16)
            load(0, 7, cols(A["w_out"][0], 0, 512))
            load(1, 7, cols(A["w_out"][0], 512, 512))
            for j in range(2):
                load(0, 8 + j, cols(A["conv_w_in_2"][0], j * 512, 512))
                load(1, 8 + j, cols(A["conv_w_in_2"][0], D + j * 512, 512))
                load(2, 7 + j, cols(A["conv_w_in_2"][0], 2 * D + j * 512, 512))
            load(0, 10, cols(A["conv_w_out_2"][0], 0, 512))
            load(1, 10, cols(A["conv_w_out_2"][0], 512, 512))

            sp.wait_ge(xn_done, 4)
            sp.dma_start(subk, A["subk"][0].rearrange("p (c n) -> p c n", c=16)).then_inc(subk_loaded, 16)
            sp.dma_start(gain_row[:], A["ffn_norm_g_2"][0].partition_broadcast(P)).then_inc(gain_loaded, 16)

            def load_queries(layer):
                (b, use), (b1, use1) = QUERY_FILLS[layer]
                load(b, use, cols(A["peer_w_q_2"][layer], 0, 512))
                for c in range(3):
                    load(b1, use1 + c, cols(A["peer_w_q_2"][layer], (c + 1) * 512, 512))

            load_queries(0)
            load(1, 11, cols(A["attn_w_qkv_2"][0], D, 512))
            sp.wait_ge(xn_done, 8)
            sp.dma_start(gain_row[:], A["ffn_norm_g_2"][1].partition_broadcast(P)).then_inc(gain_loaded, 16)
            sp.wait_ge(keys_done, ONE + 4)
            sp.dma_start(subk, A["subk"][1].rearrange("p (c n) -> p c n", c=16)).then_inc(subk_loaded, 16)
            qkv = A["attn_w_qkv_2"][0].rearrange("(k p) c -> p k c", p=P)
            with sp.Fori(0, 2) as c:
                sp.wait_ge(chunk_done[2], ONE + c + 10)
                sp.dma_start(wbuf[:, 2], qkv[:, :, bass.ds(c * 512, 512)]).then_inc(w_landed[2], 16)
            load(0, 14, cols(A["attn_w_o_2"][0], 0, 512))
            load(1, 12, cols(A["attn_w_o_2"][0], 512, 512))
            load_queries(1)
            sp.wait_ge(xn_done, 12)
            sp.dma_start(gain_row[:], A["final_norm_g_2"].partition_broadcast(P)).then_inc(gain_loaded, 16)
            for t in range(TILES):
                sp.wait_ge(xn_done, 13 + t)
                sp.dma_start(out[t * P:(t + 1) * P], xn[:, t]).then_inc(out_stored, 16)
            sp.wait_ge(out_stored, 16 * TILES)

        @block.gpsimd
        def _(pool):
            for s in counts_from_one:
                pool.sem_inc(s, ONE)
            nc.gpsimd.memset(rb[:], MASKED).then_inc(rb_cleared, 1)
            pool.wait_ge(rb_cleared, 1)
            pool.dma_start(rb[0:32, 0:24], A["rel_bias"]).then_inc(rb_loaded, 16)
            pool.dma_start(rb[0:32, 24:40], A["rel_bias_2"]).then_inc(rb_loaded, 16)
            pool.dma_start(sinks[:], A["attn_sink_2"][0].partition_broadcast(P)).then_inc(sinks_loaded, 16)
            nc.gpsimd.memset(qz[:], 0.0).then_inc(pads_zero, 1)
            pool.wait_ge(rows_copied, 2)
            pool.dma_start(bias_rows1.ap(), row1[0:HEADS1]).then_inc(rows_stored, 16)
            pool.dma_start(bias_rows2.ap(), row2[0:HEADS2]).then_inc(rows_stored, 16)
            pool.wait_ge(rows_stored, 32)
            pool.dma_start(hank1, bass.AP(bias_rows1, 0, [[1, P], [REL, HEADS1 * NG], [1, HANKEL]])).then_inc(hank1_loaded, 16)
            nc.gpsimd.memset(uT[:], 0.0).then_inc(pads_zero, 1)
            pool.wait_ge(att1_done, ONE + 16)
            pool.dma_start(wpool, A["w_pool"][0].rearrange("g c d -> c g d")).then_inc(wpool_loaded, 16)
            nc.gpsimd.memset(cu[:], 0.0).then_inc(pads_zero, 1)

            def gathers(layer):
                def half(unit, t, b):
                    n = unit * 2 + b
                    pool.wait_ge(dots_done, ONE + n)
                    pool.sem_inc(pool_waited, 1)
                    for e in range(HALF):
                        idx = expert[:, t, b * HALF + e:b * HALF + e + 1]
                        pool.indirect_dma_start(uring[:, e], None, A["peer_u_2"],
                                                bass.IndirectOffsetOnAxis(ap=idx, axis=0)).then_inc(u_landed[e], 16)
                    pool.wait_ge(v_used, ONE + n)
                    pool.sem_inc(pool_waited, 1)
                    for e in range(HALF):
                        idx = expert[:, t, b * HALF + e:b * HALF + e + 1]
                        pool.indirect_dma_start(vring[:, e], None, A["peer_v_2"],
                                                bass.IndirectOffsetOnAxis(ap=idx, axis=0)).then_inc(v_landed[e], 16)

                with pool.Fori(0, PEER_HEADS) as h:
                    for t in range(TILES):
                        unit = h * TILES + (UNITS * layer + t)
                        pool.wait_ge(expert_ready, unit + 1)
                        for b in range(2):
                            half(unit, t, b)

            gathers(0)
            pool.wait_ge(x_added, 6)
            pool.dma_start(hank2, bass.AP(bias_rows2, 0, [[1, P], [REL, HEADS2], [1, HANKEL]])).then_inc(hank2_loaded, 16)
            nc.gpsimd.memset(qz2[:], 0.0).then_inc(pads_zero, 1)
            gathers(1)

        @block.scalar
        def _(act):
            def norm(k, junk_free=None):
                for t in range(TILES):
                    nc.scalar.activation(xn[:, t], x[:, t], ACT.Square, accum_out=sumsq[:, t:t + 1]).then_inc(sumsq_done, 1)
                act.wait_ge(meansq_done, k + 1)
                nc.scalar.activation(root[:], meansq[:], ACT.Sqrt).then_inc(root_done, 1)

            def turned_out(n, gain):
                for bank in (0, 2):
                    act.wait_ge(turned, 4 * n + bank + 1)
                    for c in (2 * bank, 2 * bank + 1):
                        src = ps[bank // 2][:, (c % 4) * SEQ:(c % 4 + 1) * SEQ]
                        if gain is None:
                            last = nc.scalar.activation(hT[:, c], src, ACT.Copy)
                        else:
                            last = nc.scalar.activation(hT[:, c], src, ACT.Copy, scale=pf[:, gain + c:gain + c + 1])
                    last.then_inc(turned_act, 1)

            act.wait_ge(x_loaded, 16)
            norm(0)
            act.wait_ge(rows_done, 1)
            nc.scalar.activation(row1[0:HEADS1, 0:2], psC[0:HEADS1, :].rearrange("p (g m) -> p g m", g=2), ACT.Copy)
            nc.scalar.activation(row1[0:HEADS1, 2], psD[0:HEADS1, 0:512], ACT.Copy).then_inc(rows_copied, 1)
            nc.scalar.activation(row2[0:HEADS2], psD[0:HEADS2, 512:1024], ACT.Copy).then_inc(rows_copied, 1)
            act.wait_ge(param_loaded, 16)
            turned_out(0, PF_NORM)

            act.wait_ge(pads_zero, 1)
            with act.Fori(0, HEADS1 // 2) as i:
                act.wait_ge(chunk_done[0], ONE + i + 1)
                act.wait_ge(sc1_done, ONE + i * 4)
                for a in range(2):
                    r = slice(64 * a, 64 * a + 64)
                    last = nc.scalar.activation(qz[r, a], psA[r, 0:768].rearrange("p (g t) -> p g t", g=NG), ACT.Copy,
                                                scale=HD ** -0.5)
                last.then_inc(q1_copied, 1)

                def exp(u):
                    act.wait_ge(max1_done, i * 4 + u + 1)
                    act.wait_ge(probT1_done, ONE + i * 4 + max(u - 1, 0))
                    nc.scalar.activation(prob1[:, u % 2], ps[2 + u % 2][:, 0:768], ACT.Exp, bias=small[:, u:u + 1],
                                         accum_out=small[:, 4 + u:5 + u]).then_inc(exp1_done, 1)

                exp(0)
                exp(1)
                act.wait_ge(chunk_done[2], ONE + i + 1)
                act.wait_ge(av1_done, ONE + i * 4)
                nc.scalar.activation(v1[:], psA[:].rearrange("p (t c) -> p t c", t=TILES)[:, :, 0:NG * P], ACT.Copy)\
                    .then_inc(v1_copied, 1)
                exp(2)
                exp(3)

            for n, (b, src, dst) in enumerate(((1, psB, sig_a), (2, psC, sig_b))):
                act.wait_ge(chunk_done[b], ONE + 5)
                nc.scalar.activation(dst, src[:], ACT.Sigmoid).then_inc(sig_done, 1)

            for j in range(2):
                act.wait_ge(merged_done, j) if j else act.wait_ge(gates_done, 2)
                for n, (b, src, dst) in enumerate(((0, psA, sig_a), (1, psB, sig_b))):
                    act.wait_ge(chunk_done[b], ONE + 6 + j)
                    for m in range(4):
                        bias = pf[:, PF_BG + 8 * n + 4 * j + m:PF_BG + 8 * n + 4 * j + m + 1]
                        last = nc.scalar.activation(dst[:, m * SEQ:(m + 1) * SEQ], src[:, m * SEQ:(m + 1) * SEQ],
                                                    ACT.Sigmoid, bias=bias)
                    last.then_inc(merge_sig, 1)

            act.wait_ge(x_added, 2)
            norm(1)
            act.wait_ge(xn_done, 4)
            norm(2)
            turned_out(1, PF_CONV)

            for j in range(2):
                act.wait_ge(chunk_done[1], ONE + 9 + j)
                if j:
                    act.wait_ge(conv_done, 1)
                nc.scalar.activation(gate_c, psB[:], ACT.Copy).then_inc(gc_copied, 1)

            def peer(layer):
                n = 3 + 2 * layer
                norm(n)
                turned_out(2 + 3 * layer, None)

                def queries_out(chunk, b, use):
                    act.wait_ge(chunk_done[b], use + (ONE + 1))
                    act.wait_ge(keys_done, chunk + ONE)
                    nc.scalar.activation(pqT[:], psC[:].rearrange("p (m t) -> p m t", m=4), ACT.Copy).then_inc(pq_copied, 1)

                def scores_out(chunk):
                    act.wait_ge(keys_done, chunk + (ONE + 1))
                    act.wait_ge(topk_done, chunk * 4 + ONE)
                    nc.scalar.activation(scores[:].rearrange("p t s n -> p (t s n)"), psD[:], ACT.Copy).then_inc(scores_ready, 1)

                def softmax_exp(unit, t):
                    act.wait_ge(topk_done, unit + (ONE + 1))
                    nc.scalar.activation(gate_e, sel_v, ACT.Exp, bias=small[:, 8:9], accum_out=small[:, 9:10]).then_inc(gate_exp, 1)

                def mix(unit, t, b):
                    n = unit * 2 + b
                    e0 = b * HALF
                    act.wait_ge(dots_done, ONE + n + 1)
                    nc.scalar.activation(act_e[:, t, e0:e0 + HALF], dot[:, t, e0:e0 + HALF], ACT.Gelu).then_inc(gelu_done, 1)
                    act.wait_ge(coef_done, n + 1)
                    act.wait_ge(v_used, ONE + unit * 2)
                    for e in range(HALF):
                        nc.scalar.activation(diag[:, b, e], ident, ACT.Copy, scale=coef[:, t, e0 + e:e0 + e + 1])\
                            .then_inc(diag_done, 1)

                base = UNITS * layer
                first, (b1, use1) = QUERY_FILLS[layer]

                def chunk(c, last):
                    for k in range(4):
                        unit = c * 4 + (base + k)
                        if k == 3 and not last:
                            scores_out(c + (4 * layer + 1))
                        mix(unit, k % 2, 0)
                        if k < 3 or not last:
                            softmax_exp(unit + 1, 1 - k % 2)
                        mix(unit, k % 2, 1)
                        if k == 2 and not last:
                            queries_out(c + (4 * layer + 1), b1, c + use1)

                queries_out(4 * layer, *first)
                scores_out(4 * layer)
                softmax_exp(base, 0)
                with act.Fori(0, 3) as c:
                    chunk(c, False)
                chunk(3, True)

            act.wait_ge(x_added, 4)
            peer(0)

            act.wait_ge(x_added, 6)
            norm(4)
            turned_out(3, PF_ATT)
            act.wait_ge(chunk_done[1], ONE + 12)
            nc.scalar.activation(kT2, psC[:, 0:512], ACT.Copy).then_inc(kv2_copied, 1)
            act.wait_ge(pads_zero, 4)
            with act.Fori(0, 2) as c:
                act.wait_ge(chunk_done[2], ONE + c + 11)
                act.wait_ge(sc2_done, ONE + c * 16)
                for i in range(8):
                    to, of = slice(64 * (i // 4), 64 * (i // 4) + 64), slice(64 * (i % 2), 64 * (i % 2) + 64)
                    last = nc.scalar.activation(qz2[to, i], psA[of, (i // 2) * SEQ:(i // 2 + 1) * SEQ], ACT.Copy,
                                                scale=HD ** -0.5)
                last.then_inc(q2_copied, 1)
                for u in range(16):
                    act.wait_ge(max2_done, c * 16 + u + 1)
                    act.wait_ge(probT2_done, ONE + c * 16 + max(u - 3, 0))
                    nc.scalar.activation(prob2[:, u % 4, 0:257], ps[2 + u // 2 % 2][:, (u % 2) * 512:(u % 2) * 512 + 257], ACT.Exp,
                                         bias=small[:, 16 + u:17 + u], accum_out=small[:, 32 + u:33 + u]).then_inc(exp2_done, 1)
            turned_out(4, None)

            act.wait_ge(x_added, 8)
            peer(1)
            act.wait_ge(x_added, 10)
            norm(6)

        @block.tensor
        def _(pe):
            mm = nc.tensor.matmul

            def turn(n, src):
                for bank in range(4):
                    for c in (2 * bank, 2 * bank + 1):
                        for t in range(TILES):
                            last = nc.tensor.transpose(ps[bank // 2][:, (c % 4) * SEQ + t * P:(c % 4) * SEQ + (t + 1) * P],
                                                       src[:, t, c * P:(c + 1) * P], ident)
                    last.then_inc(turned, 1)

            def turned_in(n):
                pe.wait_ge(turned_act, 2 * n + 2)
                pe.wait_ge(turned_dve, 2 * n + 2)

            def columns(dst, b, use, src=hT, k0=0, k1=KC, count=True):
                pe.wait_ge(w_landed[b], landed_value(b, use))
                for m in range(4):
                    for k in range(k0, k1):
                        last = mm(dst[:, m * SEQ:(m + 1) * SEQ], wbuf[:, b, k, m * P:(m + 1) * P], src[:, k - k0],
                                  start=(k == k0), stop=(k == k1 - 1))
                if count:
                    last.then_inc(chunk_done[b], 1)

            def rows(dst, b, use, src):
                pe.wait_ge(w_landed[b], landed_value(b, use))
                for t in range(TILES):
                    for k in range(KC):
                        last = mm(dst[:, t * 512:(t + 1) * 512], src[:, k, t * P:(t + 1) * P], wbuf[:, b, k],
                                  start=(k == 0), stop=(k == KC - 1))
                last.then_inc(chunk_done[b], 1)

            pe.wait_ge(const_loaded, 32)
            pe.wait_ge(rb_loaded, 32)
            for n in range(4):
                heads = HEADS1 if n < NG else HEADS2
                last = mm(ps[2 + n // 2][0:heads, (n % 2) * 512:(n % 2 + 1) * 512], rb[0:33, 8 * n:8 * n + heads],
                          bucket[0:33, n * REL:(n + 1) * REL], start=True, stop=True)
            last.then_inc(rows_done, 1)

            pe.wait_ge(xn_done, 2)
            turn(0, xn)
            turned_in(0)

            pe.wait_ge(rows_copied, 2)
            pe.wait_ge(hank1_loaded, 16)
            with pe.Fori(0, HEADS1 // 2) as i:
                def project(dst, b):
                    pe.wait_ge(w_landed[b], i * 48 + 48)
                    for g in range(NG):
                        for k in range(KC):
                            last = mm(dst[:, g * SEQ:(g + 1) * SEQ], wbuf[:, b, k, g * P:(g + 1) * P], hT[:, k],
                                      start=(k == 0), stop=(k == KC - 1))
                    last.then_inc(chunk_done[b], 1)

                def score(u):
                    a, t, dst = u // 2, u % 2, ps[2 + u % 2]
                    pe.wait_ge(exp1_done, ONE + i * 4 + max(u - 1, 0))
                    for g in range(NG):
                        mm(dst[:, g * SEQ:(g + 1) * SEQ], qz[:, a, g, t * P:(t + 1) * P], kT[:, g], start=True, stop=False)
                        last = mm(dst[:, g * SEQ:(g + 1) * SEQ], reverse,
                                  arena[:, bass.ds(i * (6 * HANKEL) + ((a * NG + g) * HANKEL + P * (1 - t)), SEQ)],
                                  start=False, stop=True)
                    last.then_inc(sc1_done, 1)

                def turn_probs(u):
                    pe.wait_ge(exp1_done, ONE + i * 4 + u + 1)
                    pe.wait_ge(probT1_copied, ONE + i * 4 + u)
                    for m in range(6):
                        last = nc.tensor.transpose(psB[:, m * P:(m + 1) * P], prob1[:, u % 2, m * P:(m + 1) * P], ident)
                    last.then_inc(probT1_done, 1)

                def times_v(u):
                    a = u // 2
                    pe.wait_ge(probT1_copied, ONE + i * 4 + u + 1)
                    pe.wait_ge(att1_done, ONE + i * 4 + max(u - 1, 0))
                    for m in range(6):
                        g, kt = m // 2, m % 2
                        last = mm(psA[:, (u % 2) * 512:(u % 2) * 512 + HD], probT1[:, u % 2, m],
                                  v1[:, kt, g * P + a * HD:g * P + a * HD + HD], start=(m == 0), stop=(m == 5))
                    last.then_inc(av1_done, 1)

                pe.wait_ge(att1_done, ONE + i * 4)
                project(psA, 0)
                pe.wait_ge(probT1_copied, ONE + i * 4)
                project(psB, 1)
                pe.wait_ge(q1_copied, i + 1)
                pe.wait_ge(k1_copied, i + 1)
                score(0)
                score(1)
                pe.wait_ge(w_landed[2], i * 48 + 48)
                for t in range(TILES):
                    for k in range(KC):
                        last = mm(psA[:, t * 512:t * 512 + NG * P], hT[:, k, t * P:(t + 1) * P], wbuf[:, 2, k, 0:NG * P],
                                  start=(k == 0), stop=(k == KC - 1))
                last.then_inc(chunk_done[2], 1)
                turn_probs(0)
                score(2)
                turn_probs(1)
                pe.wait_ge(v1_copied, i + 1)
                times_v(0)
                score(3)
                turn_probs(2)
                times_v(1)
                turn_probs(3)
                times_v(2)
                times_v(3)

            pe.wait_ge(att1_done, ONE + 16)
            columns(psA, 0, 4)
            pe.wait_ge(probT1_copied, ONE + 16)
            columns(psB, 1, 4)
            pe.wait_ge(exp1_done, ONE + 16)
            columns(psC, 2, 4)
            for m in range(4):
                for t in range(TILES):
                    last = nc.tensor.transpose(psD[:, m * SEQ + t * P:m * SEQ + (t + 1) * P], att1[:, t, m * P:(m + 1) * P], ident)
            last.then_inc(att1_turned, 1)
            pe.wait_ge(pooled_done, 1)
            pe.wait_ge(wpool_loaded, 16)
            for g in range(POOL_GROUPS):
                last = mm(psA[:, g * SEQ:(g + 1) * SEQ], wpool[:, g], pooled[:, g], start=True, stop=True)
            last.then_inc(mixed_done, 1)
            for j in range(2):
                if j == 0:
                    pe.wait_ge(ya_done, 1)
                    pe.wait_ge(gates_done, 2)
                else:
                    pe.wait_ge(merge_sig, 2)
                columns(psA, 0, 5 + j)
                columns(psB, 1, 5 + j)
                if j == 0:
                    pe.wait_ge(yb_done, 1)
                else:
                    pe.wait_ge(merged_done, 1)
                columns(psC, 2, 5 + j, src=yaT, k0=0, k1=4, count=False)
                columns(psD, 2, 5 + j, src=ybT, k0=4, k1=8)
            pe.wait_ge(merge_sig, 4)
            pe.wait_ge(merged_done, 2)
            rows(psA, 0, 7, merged)
            rows(psB, 1, 7, merged)

            pe.wait_ge(x_added, 2)
            pe.wait_ge(xn_done, 6)
            turn(1, xn)
            turned_in(1)
            for j in range(2):
                if j:
                    pe.wait_ge(conv_done, 1)
                columns(psA, 0, 8 + j)
                columns(psB, 1, 8 + j)
                columns(psC, 2, 7 + j)
            pe.wait_ge(conv_done, 2)
            rows(psA, 0, 10, cT)
            rows(psB, 1, 10, cT)

            def peer(layer):
                n = 3 + 2 * layer
                pe.wait_ge(x_added, (4, 8)[layer])
                pe.wait_ge(xn_done, (8, 12)[layer])
                turn(2 + 3 * layer, xn)
                turned_in(2 + 3 * layer)
                (b0, use0), (b1, use1) = QUERY_FILLS[layer]
                columns(psC, b0, use0)

                def keys(chunk):
                    pe.wait_ge(pq_copied, chunk + 1)
                    pe.wait_ge(scores_ready, chunk) if not isinstance(chunk, int) or chunk else None
                    for t in range(TILES):
                        for m in range(4):
                            last = mm(psD[:, t * 512 + m * NKEYS:t * 512 + (m + 1) * NKEYS], pqT[:, m, t * P:(t + 1) * P],
                                      next_keys(chunk, m), start=True, stop=True)
                    last.then_inc(keys_done, 1)

                def next_keys(chunk, m):
                    c = chunk - 4 * layer
                    return subk[:, m] if isinstance(c, int) else arena[:, bass.ds(c * (4 * NKEYS) + (SUBK + m * NKEYS), NKEYS)]

                pe.wait_ge(subk_loaded, 16 * (layer + 1))
                keys(4 * layer)
                pe.wait_ge(zeros_ready, 1)
                for t in range(TILES):
                    for s in range(2):
                        mm(ps[t][:, s * 512:(s + 1) * 512], zeros, xn[:, 0, 0:512], start=True, stop=False,
                           skip_group_check=True)

                def chunk(c, last):
                    for k in range(4):
                        for b in range(2):
                            n = c * 8 + (2 * UNITS * layer + 2 * k + b)
                            m = 2 * k + b - 2
                            if not last and 0 <= m < 4:
                                if m == 0:
                                    pe.wait_ge(w_landed[b1], c * 16 + landed_value(b1, use1))
                                    pe.wait_ge(pq_copied, c + (4 * layer + 1))
                                for kc in range(KC):
                                    mq = mm(psC[:, m * SEQ:(m + 1) * SEQ], wbuf[:, b1, kc, m * P:(m + 1) * P], hT[:, kc],
                                            start=(kc == 0), stop=(kc == KC - 1))
                                if m == 3:
                                    mq.then_inc(chunk_done[b1], 1)
                            if not last and k == 3 and b == 0:
                                keys(c + (4 * layer + 1))
                            for e in range(HALF):
                                pe.wait_ge(v_landed[e], n * 16 + 16)
                                pe.wait_ge(diag_done, n * HALF + (e + 1))
                                for s in range(2):
                                    mv = mm(ps[k % 2][:, s * 512:(s + 1) * 512], diag[:, b, e], vring[:, e, s * 512:(s + 1) * 512],
                                            start=False, stop=False, skip_group_check=True)
                            mv.then_inc(v_used, 1)

                with pe.Fori(0, 3) as c:
                    chunk(c, False)
                chunk(3, True)

            peer(0)

            pe.wait_ge(x_added, 6)
            pe.wait_ge(xn_done, 10)
            turn(3, xn)
            turned_in(3)
            pe.wait_ge(w_landed[1], landed_value(1, 11))
            for m in range(2):
                for k in range(KC):
                    mm(psC[:, m * SEQ:(m + 1) * SEQ], wbuf[:, 1, k, m * P:(m + 1) * P], hT[:, k], start=(k == 0), stop=(k == KC - 1))
            for t in range(TILES):
                for k in range(KC):
                    last = mm(psC[:, 512 + t * 256:512 + (t + 1) * 256], hT[:, k, t * P:(t + 1) * P], wbuf[:, 1, k, 256:512],
                              start=(k == 0), stop=(k == KC - 1))
            last.then_inc(chunk_done[1], 1)
            pe.wait_ge(kv2_copied, 1)
            pe.wait_ge(v2_copied, 1)
            pe.wait_ge(hank2_loaded, 16)
            pe.wait_ge(sinks_loaded, 16)
            with pe.Fori(0, 2) as c:
                pe.wait_ge(w_landed[2], c * 16 + landed_value(2, 10))
                pe.wait_ge(att2_done, ONE + c * 16)
                for m in range(4):
                    for k in range(KC):
                        last = mm(psA[:, m * SEQ:(m + 1) * SEQ], wbuf[:, 2, k, m * P:(m + 1) * P], hT[:, k],
                                  start=(k == 0), stop=(k == KC - 1))
                last.then_inc(chunk_done[2], 1)
                pe.wait_ge(q2_copied, c + 1)

                def score(u):
                    i, t = u // 2, u % 2
                    dst = ps[2 + u // 2 % 2][:, (u % 2) * 512:(u % 2) * 512 + 257]
                    pe.wait_ge(exp2_done, ONE + c * 16 + max(u - 3, 0))
                    mm(dst[:, 256:257], reverse, sinks[:, bass.ds(c * 8 + i, 1)], start=True, stop=True)
                    mm(dst[:, 0:256], qz2[:, i, t * P:(t + 1) * P], kT2[:, bass.ds(c * SEQ, SEQ)], start=True, stop=False)
                    mm(dst[:, 0:256], reverse, arena[:, bass.ds(c * (8 * HANKEL) + (i * HANKEL + P * (1 - t)), SEQ)],
                       start=False, stop=True).then_inc(sc2_done, 1)

                def turn_probs(u):
                    pe.wait_ge(exp2_done, ONE + c * 16 + u + 1)
                    pe.wait_ge(probT2_copied, ONE + c * 16 + max(u - 1, 0))
                    for kt in range(2):
                        last = nc.tensor.transpose(psB[:, (u % 2) * 512 + kt * P:(u % 2) * 512 + (kt + 1) * P],
                                                   prob2[:, u % 4, kt * P:(kt + 1) * P], ident)
                    last.then_inc(probT2_done, 1)

                def times_v(u):
                    i = u // 2
                    pe.wait_ge(probT2_copied, ONE + c * 16 + u + 1)
                    pe.wait_ge(att2_done, ONE + c * 16 + max(u - 1, 0))
                    for kt in range(2):
                        last = mm(psA[:, (u % 2) * 512:(u % 2) * 512 + HD], probT2[:, u % 4, kt],
                                  v2[:, kt, bass.ds(c * P + (i // 4) * HD, HD)], start=(kt == 0), stop=(kt == 1))
                    last.then_inc(av2_done, 1)

                for s in range(16 + 3):
                    if s < 16:
                        score(s)
                    if 0 <= s - 2 < 16:
                        turn_probs(s - 2)
                    if 0 <= s - 3 < 16:
                        times_v(s - 3)
            pe.wait_ge(att2_done, ONE + 32)
            turn(4, att2)
            turned_in(4)
            rows(psA, 0, 14, hT)
            rows(psB, 1, 12, hT)
            peer(1)

        @block.vector
        def _(dve):
            class Chain:
                first, n = 0, 0

                def link(self, ins):
                    self.n += 1
                    ins.then_inc(dve_step, 1)
                    dve.wait_ge(dve_step, self.first + self.n)

                def loop(self, i, per):
                    self.before, self.first, self.n, self.per = self.first + self.n, i * per + (self.first + self.n), 0, per

                def end(self, times):
                    assert self.n == self.per, self.n
                    self.first, self.n = self.before + times * self.per, 0

            chain = Chain()
            link = chain.link

            def norm(k):
                dve.wait_ge(sumsq_done, 2 * k + 2)
                nc.vector.tensor_scalar(meansq[:], sumsq[:], 1.0 / D, EPS, ALU.mult, ALU.add).then_inc(meansq_done, 1)
                dve.wait_ge(meansq_done, k + 1)
                dve.wait_ge(root_done, k + 1)
                link(nc.vector.reciprocal(root[:], root[:]))
                link(nc.vector.tensor_tensor(rinv[:], root[:], root[:], ALU.mult))
                link(nc.vector.tensor_tensor(rinv[:], rinv[:], meansq[:], ALU.mult))
                link(nc.vector.tensor_scalar(rinv[:], rinv[:], -0.5, 1.5, ALU.mult, ALU.add))
                link(nc.vector.tensor_tensor(rinv[:], rinv[:], root[:], ALU.mult))

            def plain(k):
                norm(k)
                for t in range(TILES):
                    nc.vector.tensor_scalar(xn[:, t], x[:, t], rinv[:, t:t + 1], None, ALU.mult).then_inc(xn_done, 1)

            def with_gain(k, gains, dst):
                norm(k)
                dve.wait_ge(gain_loaded, 16 * gains)
                for t in range(TILES):
                    nc.vector.scalar_tensor_tensor(out=dst[:, t], in0=x[:, t], scalar=rinv[:, t:t + 1], in1=gain_row[:],
                                                   op0=ALU.mult, op1=ALU.mult).then_inc(xn_done, 1)

            def turned_out(n, gain):
                for bank in (1, 3):
                    dve.wait_ge(turned, 4 * n + bank + 1)
                    for c in (2 * bank, 2 * bank + 1):
                        src = ps[bank // 2][:, (c % 4) * SEQ:(c % 4 + 1) * SEQ]
                        if gain is None:
                            last = nc.vector.tensor_copy(hT[:, c], src)
                        else:
                            last = nc.vector.tensor_scalar(hT[:, c], src, pf[:, gain + c:gain + c + 1], None, ALU.mult)
                    last.then_inc(turned_dve, 1)

            def residual(added, waits):
                for j, (s, value) in enumerate(waits):
                    dve.wait_ge(s, value)
                    dst = x[:, :, j * 512:(j + 1) * 512]
                    nc.vector.tensor_tensor(dst, ps[j][:].rearrange("p (t c) -> p t c", t=TILES), dst, ALU.add).then_inc(x_added, 1)

            nc.vector.memset(zeros, 0.0).then_inc(zeros_ready, 1)
            plain(0)
            dve.wait_ge(param_loaded, 16)
            turned_out(0, PF_NORM)

            with dve.Fori(0, HEADS1 // 2) as i:
                chain.loop(i, 4)
                dve.wait_ge(chunk_done[1], ONE + i + 1)
                dve.wait_ge(sc1_done, ONE + i * 4)
                nc.vector.tensor_copy(kT[:], psB[:, 0:768].rearrange("p (g t) -> p g t", g=NG)).then_inc(k1_copied, 1)

                def row_max(u):
                    dve.wait_ge(sc1_done, ONE + i * 4 + u + 1)
                    dve.wait_ge(exp1_done, ONE + i * 4 + max(u - 1, 0))
                    nc.vector.tensor_reduce(small[:, u:u + 1], ps[2 + u % 2][:, 0:768], AX_X, ALU.max, negate=True)\
                        .then_inc(max1_done, 1)

                def copy_probs(u):
                    dve.wait_ge(probT1_done, ONE + i * 4 + u + 1)
                    dve.wait_ge(av1_done, ONE + i * 4 + max(u - 1, 0))
                    nc.vector.tensor_copy(probT1[:, u % 2], psB[:, 0:768].rearrange("p (m t) -> p m t", m=6))\
                        .then_inc(probT1_copied, 1)

                def output(u):
                    a, t = u // 2, u % 2
                    link(nc.vector.reciprocal(small[:, 10 + u:11 + u], small[:, 4 + u:5 + u]))
                    dve.wait_ge(av1_done, ONE + i * 4 + u + 1)
                    nc.vector.tensor_scalar(att1[:, t, bass.ds(i * P + a * HD, HD)], psA[:, (u % 2) * 512:(u % 2) * 512 + HD],
                                            small[:, 10 + u:11 + u], None, ALU.mult).then_inc(att1_done, 1)

                row_max(0)
                row_max(1)
                copy_probs(0)
                row_max(2)
                copy_probs(1)
                output(0)
                row_max(3)
                copy_probs(2)
                output(1)
                copy_probs(3)
                output(2)
                output(3)
            chain.end(HEADS1 // 2)

            dve.wait_ge(pads_zero, 2)
            dve.wait_ge(chunk_done[0], ONE + 5)
            link(nc.vector.tensor_copy(uT[:, :, PAD:PAD + SEQ], psA[:].rearrange("p (g t) -> p g t", g=4)))

            def window(dst, src, g, lo, hi, shift):
                left = 1 if shift == 0 else shift
                link(nc.vector.tensor_tensor(dst[:, g:4, PAD + lo:PAD + hi], src[:, g:4, PAD + lo - left:PAD + hi - left],
                                             src[:, g:4, PAD + lo + shift:PAD + hi + shift], ALU.add))

            window(win2, uT, 0, -7, SEQ + 7, 0)
            window(win4, win2, 1, -6, SEQ + 6, 1)
            window(win8, win4, 2, -4, SEQ + 4, 2)
            window(win2, win8, 3, 0, SEQ, 4)
            sums = (win2, win4, win8, win2)
            for g in range(4):
                last = nc.vector.tensor_tensor(pooled[:, g], sums[g][:, g, PAD:PAD + SEQ], inv_count[:, g], ALU.mult)
            link(last)
            nc.vector.tensor_tensor(pooled[:], pooled[:], uT[:, :, PAD:PAD + SEQ], ALU.subtract).then_inc(pooled_done, 1)

            dve.wait_ge(sig_done, 1)
            nc.vector.tensor_tensor(gate_a, psB[:], sig_a, ALU.mult).then_inc(gates_done, 1)
            dve.wait_ge(sig_done, 2)
            nc.vector.tensor_tensor(gate_b, psC[:], sig_b, ALU.mult).then_inc(gates_done, 1)
            dve.wait_ge(gates_done, 2)
            dve.wait_ge(att1_turned, 1)
            nc.vector.tensor_tensor(ybT[:].rearrange("p m t -> p (m t)"), psD[:], gate_b, ALU.mult).then_inc(yb_done, 1)
            dve.wait_ge(mixed_done, 1)
            for g in range(POOL_GROUPS):
                last = nc.vector.scalar_tensor_tensor(out=yaT[:, g], in0=psA[:, g * SEQ:(g + 1) * SEQ],
                                                      scalar=pf[:, PF_POOL + g:PF_POOL + g + 1],
                                                      in1=gate_a[:, g * SEQ:(g + 1) * SEQ], op0=ALU.mult, op1=ALU.mult)
            last.then_inc(ya_done, 1)
            for j in range(2):
                dve.wait_ge(merge_sig, 2 * j + 2)
                dve.wait_ge(chunk_done[2], ONE + 6 + j)
                nc.vector.tensor_tensor(prod_a, psC[:], sig_a, ALU.mult)
                link(nc.vector.tensor_tensor(prod_b, psD[:], sig_b, ALU.mult))
                nc.vector.tensor_tensor(merged[:, 4 * j:4 * j + 4].rearrange("p m t -> p (m t)"), prod_a, prod_b, ALU.add)\
                    .then_inc(merged_done, 1)
            dve.wait_ge(merged_done, 2)
            residual(2, ((chunk_done[0], ONE + 8), (chunk_done[1], ONE + 8)))
            dve.wait_ge(x_added, 2)
            with_gain(1, 1, x)
            dve.wait_ge(xn_done, 4)
            plain(2)
            turned_out(1, PF_CONV)

            dve.wait_ge(pads_zero, 3)
            for j in range(2):
                dve.wait_ge(gc_copied, j + 1)
                dve.wait_ge(chunk_done[2], ONE + 8 + j)
                link(nc.vector.tensor_tensor(cu[:, :, 1:1 + SEQ], psC[:].rearrange("p (m t) -> p m t", m=4),
                                             gate_c.rearrange("p (m t) -> p m t", m=4), ALU.mult))
                for tap in range(3):
                    for m in range(4):
                        w = pf[:, PF_CW + tap * KC + 4 * j + m:PF_CW + tap * KC + 4 * j + m + 1]
                        if tap == 0:
                            last = nc.vector.tensor_scalar(cacc[:, m], cu[:, m, 0:SEQ], w, None, ALU.mult)
                        else:
                            last = nc.vector.scalar_tensor_tensor(out=cacc[:, m], in0=cu[:, m, tap:tap + SEQ], scalar=w,
                                                                  in1=cacc[:, m], op0=ALU.mult, op1=ALU.add)
                    link(last)
                dve.wait_ge(chunk_done[0], ONE + 9 + j)
                nc.vector.tensor_tensor(cT[:, 4 * j:4 * j + 4], psA[:].rearrange("p (m t) -> p m t", m=4), cacc[:], ALU.mult)\
                    .then_inc(conv_done, 1)
                dve.wait_ge(conv_done, j + 1)
            residual(4, ((chunk_done[0], ONE + 11), (chunk_done[1], ONE + 11)))

            def peer(layer):
                dve.wait_ge(x_added, (4, 8)[layer])
                with_gain(3 + 2 * layer, 2 + layer, xn)
                turned_out(2 + 3 * layer, None)

                def apart():
                    dve.sem_inc(dve_waited, 1)

                def linked(ins):
                    link(ins)
                    apart()

                def top16(values, indices, src, n):
                    for p in range(n):
                        last = nc.vector.max(values(p, 0), src(p))
                    linked(last)
                    for p in range(n):
                        last = nc.vector.max_index(indices(p, 0), values(p, 0), src(p))
                    linked(last)
                    for p in range(n):
                        last = nc.vector.match_replace(src(p), values(p, 0), src(p), LOWEST)
                    linked(last)
                    for p in range(n):
                        last = nc.vector.max(values(p, 1), src(p))
                    linked(last)
                    for p in range(n):
                        last = nc.vector.max_index(indices(p, 1), values(p, 1), src(p))
                    linked(last)

                def topk(unit, t, head, chunk=None):
                    if chunk is not None:
                        dve.wait_ge(scores_ready, chunk + 1)
                        apart()
                    top16(lambda p, r: top_v[:, p, 8 * r:8 * r + 8], lambda p, r: top_i[:, p, 8 * r:8 * r + 8],
                          lambda p: scores[:, t, 2 * head + p], 2)
                    grid = cand.rearrange("p (a b) -> p a b", a=TOPK)
                    linked(nc.vector.tensor_tensor(grid, top_v[:, 0].unsqueeze(2).to_broadcast([P, TOPK, TOPK]),
                                                 top_v[:, 1].unsqueeze(1).to_broadcast([P, TOPK, TOPK]), ALU.add))
                    top16(lambda p, r: sel_v[:, 8 * r:8 * r + 8], lambda p, r: sel_p[:, 8 * r:8 * r + 8], lambda p: cand, 1)
                    nc.vector.tensor_scalar(small[:, 8:9], sel_v[:, 0:1], -1.0, None, ALU.mult).then_inc(topk_done, 1)
                    nc.vector.tensor_scalar(sel_i, sel_p, 4, None, ALU.logical_shift_right)
                    link(nc.vector.tensor_scalar(sel_j, sel_p, 15, None, ALU.bitwise_and))
                    for p, sel in enumerate((sel_i, sel_j)):
                        last = nc.vector.tensor_tensor(onehot[:, p], sel.unsqueeze(2).to_broadcast([P, TOPK, TOPK]),
                                                       iota16.unsqueeze(1).to_broadcast([P, TOPK, TOPK]), ALU.is_equal)
                    link(last)
                    for p in range(2):
                        last = nc.vector.tensor_tensor(onehot[:, p], onehot[:, p],
                                                       top_i[:, p].unsqueeze(1).to_broadcast([P, TOPK, TOPK]), ALU.mult)
                    link(last)
                    link(nc.vector.tensor_reduce(key_ij[:], onehot[:], AX_X, ALU.add))
                    link(nc.vector.tensor_scalar(key_ij[:, 0], key_ij[:, 0], float(NKEYS), float(EXPERTS * layer), ALU.mult, ALU.add))
                    dve.wait_ge(v_used, ONE + 2 * unit - 2 if not isinstance(unit, int) else max(2 * unit - 2, 0))
                    nc.vector.tensor_tensor(expert[:, t], key_ij[:, 0], key_ij[:, 1], ALU.add).then_inc(expert_ready, 1)
                    dve.wait_ge(gate_exp, unit + 1)
                    link(nc.vector.reciprocal(small[:, 14:15], small[:, 9:10]))
                    link(nc.vector.tensor_scalar(gate[:, t], gate_e, small[:, 14:15], None, ALU.mult))

                STEPS = 18

                def dots(unit, t, b):
                    n = unit * 2 + b
                    for e in range(HALF):
                        dve.wait_ge(u_landed[e], n * 16 + 16)
                        last = nc.vector.tensor_tensor_reduce(out=uring[:, e], in0=xn[:, t], in1=uring[:, e], scale=1.0,
                                                              scalar=0.0, op0=ALU.mult, op1=ALU.add,
                                                              accum_out=dot[:, t, b * HALF + e:b * HALF + e + 1])
                    last.then_inc(dots_done, 1)

                def coefs(unit, t, b):
                    n = unit * 2 + b
                    dve.wait_ge(gelu_done, n + 1)
                    e = slice(b * HALF, (b + 1) * HALF)
                    nc.vector.tensor_tensor(coef[:, t, e], act_e[:, t, e], gate[:, t, e], ALU.mult).then_inc(coef_done, 1)

                base = UNITS * layer

                def chunk(c, last):
                    for k in range(4):
                        unit = c * 4 + (base + k)
                        dots(unit, k % 2, 0)
                        coefs(unit, k % 2, 0)
                        if k < 3:
                            topk(unit + 1, (k + 1) % 2, (k + 1) // 2)
                        elif not last:
                            topk(unit + 1, 0, 0, c + (4 * layer + 1))
                        dots(unit, k % 2, 1)
                        coefs(unit, k % 2, 1)

                topk(base, 0, 0, 4 * layer)
                with dve.Fori(0, 3) as c:
                    chain.loop(c, 4 * STEPS)
                    chunk(c, False)
                chain.end(3)
                chunk(3, True)
                for t in range(TILES):
                    dve.wait_ge(v_used, ONE + 2 * UNITS * (layer + 1))
                    nc.vector.tensor_tensor(x[:, t], ps[t][:], x[:, t], ALU.add).then_inc(x_added, 1)

            peer(0)

            dve.wait_ge(x_added, 6)
            plain(4)
            turned_out(3, PF_ATT)
            dve.wait_ge(chunk_done[1], ONE + 12)
            nc.vector.tensor_copy(v2[:], psC[:, 512:1024].rearrange("p (t c) -> p t c", t=TILES)).then_inc(v2_copied, 1)
            with dve.Fori(0, 2) as c:
                chain.loop(c, 16)

                def row_max(u):
                    dve.wait_ge(sc2_done, ONE + c * 16 + u + 1)
                    nc.vector.tensor_reduce(small[:, 16 + u:17 + u], ps[2 + u // 2 % 2][:, (u % 2) * 512:(u % 2) * 512 + 257],
                                            AX_X, ALU.max, negate=True).then_inc(max2_done, 1)

                def copy_probs(u):
                    dve.wait_ge(probT2_done, ONE + c * 16 + u + 1)
                    dve.wait_ge(av2_done, ONE + c * 16 + max(u - 3, 0))
                    nc.vector.tensor_copy(probT2[:, u % 4], psB[:, (u % 2) * 512:(u % 2) * 512 + 256].rearrange(
                        "p (m t) -> p m t", m=2)).then_inc(probT2_copied, 1)

                def output(u):
                    i, t = u // 2, u % 2
                    link(nc.vector.reciprocal(small[:, 48 + u % 2:49 + u % 2], small[:, 32 + u:33 + u]))
                    dve.wait_ge(av2_done, ONE + c * 16 + u + 1)
                    nc.vector.tensor_scalar(att2[:, t, bass.ds(c * 512 + i * HD, HD)], psA[:, (u % 2) * 512:(u % 2) * 512 + HD],
                                            small[:, 48 + u % 2:49 + u % 2], None, ALU.mult).then_inc(att2_done, 1)

                for s in range(16 + 3):
                    if s < 16:
                        row_max(s)
                    if 0 <= s - 2 < 16:
                        copy_probs(s - 2)
                    if 0 <= s - 3 < 16:
                        output(s - 3)
            chain.end(2)
            turned_out(4, None)
            residual(8, ((chunk_done[0], ONE + 15), (chunk_done[1], ONE + 13)))
            peer(1)
            dve.wait_ge(x_added, 10)
            with_gain(6, 4, xn)


def kernel(**inputs):
    import concourse.bacc as bacc
    from concourse.bass_utils import run_bass_kernel_spmd

    def raw(name):
        return np.ascontiguousarray(inputs[name])

    def feature_columns(v):
        return np.ascontiguousarray(np.reshape(v, (-1, P)).T)

    arrays = {n: raw(n) for n in ("x", "w_in", "rel_bias", "w_pool", "w_proj_a", "w_proj_b", "w_out", "final_gain",
                                  "conv_w_in_2", "conv_w_out_2", "attn_w_qkv_2", "attn_sink_2", "attn_w_o_2",
                                  "rel_bias_2", "ffn_norm_g_2", "peer_w_q_2", "final_norm_g_2")}
    for n in ("peer_u_2", "peer_v_2"):
        arrays[n] = raw(n).reshape(2 * EXPERTS, D)
    arrays["subk"] = np.ascontiguousarray(raw("peer_subkeys_2").transpose(0, 4, 1, 2, 3).reshape(2, P, 16 * NKEYS))
    arrays["pf"] = np.concatenate([feature_columns(raw(n)) for n in (
        "norm_gain", "conv_norm_g_2", "attn_norm_g_2", "pool_scale", "b_gate", "conv_w_2")], axis=1)
    arrays["const"] = constants()
    arrays["bucket"] = bucket_table()

    nc = bacc.Bacc("TRN2", target_bir_lowering=False, num_devices=1)
    aps = {n: nc.dram_tensor(f"in_{n}", a.shape, mybir.dt.from_np(a.dtype), kind="ExternalInput").ap()
           for n, a in arrays.items()}
    out = nc.dram_tensor("out", (SEQ, D), F32, kind="ExternalOutput").ap()
    build(nc, aps, out)
    r = run_bass_kernel_spmd(nc, [{f"in_{n}": a for n, a in arrays.items()}], core_ids=[0])
    return r.results[0]["out"].reshape(1, SEQ, D)
```

```python
from contextlib import ExitStack

import numpy as np

import concourse.bass as bass
from concourse import mybir

F32 = mybir.dt.float32
U32 = mybir.dt.uint32
ALU = mybir.AluOpType
ACT = mybir.ActivationFunctionType
AX_X = mybir.AxisListType.X

P = 128
SEQ = 256
D = 1024
TILES = SEQ // P
KC = D // P
EPS = 1e-6
MASKED = -1e30
ONE = 1
LOWEST = -3e38

BRANCH = 512
A_IN, A_GATE, Q1, K1, V1, B_GATE, G_LOG = 0, 512, 1024, 2560, 4096, 5632, 6144
GROUPS = ((128, 1), (512, 4), (2048, 16))
NG = len(GROUPS)
HEADS1 = 8
HD = 64
POOL_GROUPS = 4
REL = 512
HANKEL = 384

HEADS2 = 16
WINDOW2 = 128
PEER_HEADS = 8
NKEYS = 128
TOPK = 16
EXPERTS = NKEYS * NKEYS
UNITS = PEER_HEADS * TILES
HALF = TOPK // 2

PF_NORM, PF_CONV, PF_ATT, PF_POOL, PF_BG, PF_CW = 0, 8, 16, 24, 28, 44
PF_ALL = 68
C_ID, C_INV, C_IOTA = 0, 128, 1152
C_ALL = 1168

FILLS = ([3] * 4 + [1] * 14, [3] * 4 + [1] * 9, [3] * 4 + [1] + [2] * 2 + [1] * 6)
QUERY_FILLS = (((0, 10), (0, 11)), ((2, 12), (0, 15)))
MIXER_FILLS = (((0, 7), (1, 7)), ((1, 10), (2, 9)), ((0, 14), (1, 12)))
NORMS = [(0, 0), (0, 1), (1, 0), (2, 0), (1, 1), (2, 1), (3, 0), (3, 1), (4, 0), (4, 1), (5, 0), (5, 1), (6, 0), (6, 1)]


def landed_value(b, use):
    return 16 * sum(FILLS[b][:use + 1])


def step(norm, tile):
    return NORMS.index((norm, tile)) + 1


def buckets(rel, far):
    n = np.abs(rel)
    nf = np.maximum(n, 1).astype(np.float32)
    large = 8 + (np.log(nf / np.float32(8)) / np.float32(np.log(far / 8)) * np.float32(8)).astype(np.int32)
    return np.where(rel > 0, 16, 0) + np.where(n < 8, n, np.minimum(large, 15))


def bucket_table():
    rel = (SEQ - 1) - np.arange(REL)
    inside = np.abs(rel) < SEQ
    rows = []
    for window, dil in GROUPS:
        rows.append(np.where(inside & (rel % dil == 0) & (np.abs(rel) <= window // 2), buckets(rel, 1024), 32))
    rows.append(np.where(inside & (np.abs(rel) <= WINDOW2), buckets(rel, 128), 32))
    return (np.arange(33)[:, None] == np.concatenate(rows)[None, :]).astype(np.float32)


def constants():
    c = np.zeros((P, C_ALL), np.float32)
    c[:, C_ID:C_ID + P] = np.eye(P)
    pos = np.arange(SEQ)
    for g in range(POOL_GROUPS):
        half = 1 << g
        count = np.minimum(pos + half - 1, SEQ - 1) - np.maximum(pos - half, 0) + 1
        c[:, C_INV + g * SEQ:C_INV + (g + 1) * SEQ] = np.float32(1) / count.astype(np.float32)
    c[:, C_IOTA:C_IOTA + TOPK] = np.arange(TOPK)
    return c


def build(nc, A, out):
    with ExitStack() as ctx:
        def sb(name, shape, dt=F32):
            return ctx.enter_context(nc.sbuf_tensor(name, shape, dt))

        def sem(name):
            return ctx.enter_context(nc.semaphore(name))

        bias_rows1 = nc.dram_tensor("bias_rows1", [HEADS1, NG, REL], F32)
        bias_rows2 = nc.dram_tensor("bias_rows2", [HEADS2, REL], F32)

        ps = [ctx.enter_context(nc.psum_tensor(f"ps{i}", [P, 1024], F32)) for i in range(4)]
        psA, psB, psC, psD = ps
        wbuf = sb("wbuf", [P, 3, KC, 512])
        x = sb("x", [P, TILES, D])
        xn = sb("xn", [P, TILES, D])
        hT = sb("hT", [P, KC, SEQ])
        gain_row = sb("gain_row", [P, D])
        pf = sb("pf", [P, PF_ALL])
        const = sb("const", [P, C_ALL])
        rb = sb("rb", [P, 24 + HEADS2])
        sinks = sb("sinks", [P, HEADS2])
        sumsq = sb("sumsq", [P, TILES])
        meansq = sb("meansq", [P, TILES])
        root = sb("root", [P, TILES])
        rinv = sb("rinv", [P, TILES])
        small = sb("small", [P, 64])
        arena = sb("arena", [P, 30720])

        ident = const[:, C_ID:C_ID + P]
        inv_count = const[:, C_INV:C_INV + 4 * SEQ].rearrange("p (g t) -> p g t", g=4)
        iota16 = const[:, C_IOTA:C_IOTA + TOPK]

        def at(first, *shape):
            n = int(np.prod(shape))
            v = arena[:, first:first + n]
            if len(shape) == 2:
                v = v.rearrange("p (a b) -> p a b", a=shape[0])
            elif len(shape) == 3:
                v = v.rearrange("p (a b c) -> p a b c", a=shape[0], b=shape[1])
            return v

        bias1 = at(0, 24, HANKEL)
        qz = at(9216, 2, NG, SEQ)
        kT = at(10752, NG, SEQ)
        v1 = at(11520, TILES, NG * P)
        prob1 = at(12288, 2, 768)
        probT1 = at(13824, 2, 6, P)
        att1 = at(15360, TILES, BRANCH)
        bucket = at(16384, 4 * REL)
        row1 = at(18432, NG, REL)
        row2 = at(19968, REL)
        hank1 = at(20480, 24, HANKEL)
        PAD = 8
        uT = at(16384, 4, SEQ + 2 * PAD)
        win2 = at(17472, 4, SEQ + 2 * PAD)
        win4 = at(18560, 4, SEQ + 2 * PAD)
        win8 = at(19648, 4, SEQ + 2 * PAD)
        pooled = at(20736, 4, SEQ)
        gate_a = at(21760, 4 * SEQ)
        gate_b = at(22784, 4 * SEQ)
        sig_a = at(23808, 4 * SEQ)
        sig_b = at(24832, 4 * SEQ)
        yaT = at(25856, 4, SEQ)
        ybT = at(26880, 4, SEQ)
        prod_a = at(0, 4 * SEQ)
        prod_b = at(1024, 4 * SEQ)
        merged = at(2048, KC, SEQ)
        wpool = at(4096, 4, P)
        gate_c = at(4608, 4 * SEQ)
        cu = at(5632, 4, SEQ + 2)
        cacc = at(6664, 4, SEQ)
        cT = at(7688, KC, SEQ)
        uring = at(0, HALF, D)
        vring = at(8192, HALF, D)
        pqT = at(16384, 4, SEQ)
        scores = at(17408, TILES, 4, NKEYS)
        diag = at(20480, 2, HALF, P)
        cand = at(23040, TOPK * TOPK)
        onehot = at(23296, 2, TOPK, TOPK)
        top_v = at(23808, 2, TOPK)
        top_i = at(23840, 2, TOPK).bitcast(U32)
        sel_v = at(23872, TOPK)
        sel_p = at(23888, TOPK).bitcast(U32)
        sel_i = at(23904, TOPK).bitcast(U32)
        sel_j = at(23920, TOPK).bitcast(U32)
        key_ij = at(23936, 2, TOPK)
        expert = at(23968, 2, TOPK).bitcast(U32)
        gate_e = at(24000, TOPK)
        gate = at(24016, 2, TOPK)
        dot = at(24048, 2, TOPK)
        act_e = at(24080, 2, TOPK)
        coef = at(24112, 2, TOPK)
        SUBK = 28672
        subk = at(SUBK, 16, NKEYS)
        bias2 = at(0, HEADS2, HANKEL)
        hank2 = at(13344, HEADS2, HANKEL)
        qz2 = at(6144, 8, SEQ)
        kT2 = at(8192, 2 * SEQ)
        v2 = at(8704, TILES, 256)
        prob2 = at(9216, 4, 264)
        probT2 = at(10272, 4, 2, P)
        att2 = at(11296, TILES, D)
        zeros = at(28544, P)

        x_loaded = [sem(f"x_loaded{t}") for t in range(TILES)]
        const_loaded = sem("const_loaded")
        param_loaded = sem("param_loaded")
        sinks_loaded = sem("sinks_loaded")
        rb_cleared = sem("rb_cleared")
        rb_loaded = sem("rb_loaded")
        pads_zero = sem("pads_zero")
        zeros_ready = sem("zeros_ready")
        rows_done = sem("rows_done")
        rows_copied = sem("rows_copied")
        rows_stored = sem("rows_stored")
        hank1_loaded = sem("hank1_loaded")
        hank2_loaded = sem("hank2_loaded")
        gain_loaded = sem("gain_loaded")
        subk_loaded = sem("subk_loaded")
        wpool_loaded = sem("wpool_loaded")
        w_landed = [sem(f"w_landed{b}") for b in range(3)]
        chunk_done = [sem(f"chunk_done{b}") for b in range(3)]
        sumsq_done = sem("sumsq_done")
        meansq_done = sem("meansq_done")
        root_done = sem("root_done")
        xn_done = sem("xn_done")
        tile_turned = sem("tile_turned")
        tile_turned_act = sem("tile_turned_act")
        tile_turned_dve = sem("tile_turned_dve")
        dve_step = sem("dve_step")
        q1_copied = sem("q1_copied")
        k1_copied = sem("k1_copied")
        v1_copied = sem("v1_copied")
        sc1_done = sem("sc1_done")
        max1_done = sem("max1_done")
        exp1_done = sem("exp1_done")
        probT1_done = sem("probT1_done")
        probT1_copied = sem("probT1_copied")
        av1_done = sem("av1_done")
        att1_done = sem("att1_done")
        sig_done = sem("sig_done")
        gates_done = sem("gates_done")
        pooled_done = sem("pooled_done")
        mixed_done = sem("mixed_done")
        att1_turned = sem("att1_turned")
        ya_done = sem("ya_done")
        yb_done = sem("yb_done")
        merge_sig = sem("merge_sig")
        merged_done = sem("merged_done")
        x_added = sem("x_added")
        gc_copied = sem("gc_copied")
        conv_done = sem("conv_done")
        kv2_copied = sem("kv2_copied")
        v2_copied = sem("v2_copied")
        q2_copied = sem("q2_copied")
        sc2_done = sem("sc2_done")
        max2_done = sem("max2_done")
        exp2_done = sem("exp2_done")
        probT2_done = sem("probT2_done")
        probT2_copied = sem("probT2_copied")
        av2_done = sem("av2_done")
        att2_done = sem("att2_done")
        pq_copied = sem("pq_copied")
        mixer_out = sem("mixer_out")
        keys_done = sem("keys_done")
        scores_ready = sem("scores_ready")
        first_queries = sem("first_queries")
        first_copied = sem("first_copied")
        first_keys = sem("first_keys")
        first_scores = sem("first_scores")
        topk_done = sem("topk_done")
        gate_exp = sem("gate_exp")
        expert_ready = sem("expert_ready")
        u_landed = [sem(f"u_landed{e}") for e in range(HALF)]
        v_landed = [sem(f"v_landed{e}") for e in range(HALF)]
        dots_done = sem("dots_done")
        gelu_done = sem("gelu_done")
        coef_done = sem("coef_done")
        diag_done = sem("diag_done")
        v_used = sem("v_used")
        out_stored = sem("out_stored")
        dve_waited = sem("dve_waited")
        pool_waited = sem("pool_waited")

        counts_from_one = [*chunk_done, sc1_done, exp1_done, probT1_done, probT1_copied, av1_done,
                           att1_done, sc2_done, exp2_done, probT2_done, probT2_copied,
                           av2_done, att2_done, dots_done, v_used, keys_done, topk_done]

        w_in = A["w_in"][0].rearrange("(k p) c -> p k c", p=P)

        def cols(w, first, n):
            return w.rearrange("(k p) c -> p k c", p=P)[:, :, first:first + n]

        TURNED_TO = ((psA, psB), (psC, psD), (psD, psA), (psC, psD), (psA, psB), (psD, psA))

        def tile_columns(n, t):
            return TURNED_TO[n][t][:].rearrange("p (c t) -> p c t", c=KC)

        block = ctx.enter_context(nc.Block())

        @block.sync
        def _(sp):
            for t in range(TILES):
                sp.dma_start(x[:, t], A["x"][0, t * P:(t + 1) * P]).then_inc(x_loaded[t], 16)
            sp.dma_start(const[:], A["const"]).then_inc(const_loaded, 16)
            sp.dma_start(bucket[0:33], A["bucket"]).then_inc(const_loaded, 16)
            sp.dma_start(pf[:], A["pf"]).then_inc(param_loaded, 16)
            sp.dma_start(gain_row[:], A["final_gain"].partition_broadcast(P)).then_inc(gain_loaded, 16)

            with sp.Fori(0, HEADS1 // 2) as i:
                for b, first in enumerate((Q1, K1, V1)):
                    sp.wait_ge(chunk_done[b], ONE + i)
                    for g in range(NG):
                        sp.dma_start(wbuf[:, b, :, g * P:(g + 1) * P],
                                     w_in[:, :, bass.ds(i * P + (first + g * 512), P)]).then_inc(w_landed[b], 16)

            def load(b, use, src):
                sp.wait_ge(chunk_done[b], ONE + use)
                sp.dma_start(wbuf[:, b], src).then_inc(w_landed[b], 16)

            load(0, 4, w_in[:, :, A_IN:A_IN + 512])
            load(1, 4, w_in[:, :, A_GATE:A_GATE + 512])
            load(2, 4, w_in[:, :, B_GATE:B_GATE + 512])
            for j in range(2):
                load(0, 5 + j, w_in[:, :, G_LOG + j * 512:G_LOG + (j + 1) * 512])
                load(1, 5 + j, w_in[:, :, G_LOG + D + j * 512:G_LOG + D + (j + 1) * 512])
                sp.wait_ge(chunk_done[2], ONE + 5 + j)
                sp.dma_start(wbuf[:, 2, 0:4], cols(A["w_proj_a"][0], j * 512, 512)).then_inc(w_landed[2], 16)
                sp.dma_start(wbuf[:, 2, 4:8], cols(A["w_proj_b"][0], j * 512, 512)).then_inc(w_landed[2], 16)
            load(0, 7, cols(A["w_out"][0], 0, 512))
            load(1, 7, cols(A["w_out"][0], 512, 512))
            for j in range(2):
                load(0, 8 + j, cols(A["conv_w_in_2"][0], j * 512, 512))
                load(1, 8 + j, cols(A["conv_w_in_2"][0], D + j * 512, 512))
                load(2, 7 + j, cols(A["conv_w_in_2"][0], 2 * D + j * 512, 512))
            load(1, 10, cols(A["conv_w_out_2"][0], 0, 512))
            load(2, 9, cols(A["conv_w_out_2"][0], 512, 512))

            sp.wait_ge(xn_done, step(1, 1))
            sp.dma_start(subk, A["subk"][0].rearrange("p (c n) -> p c n", c=16)).then_inc(subk_loaded, 16)
            sp.dma_start(gain_row[:], A["ffn_norm_g_2"][0].partition_broadcast(P)).then_inc(gain_loaded, 16)

            def load_queries(layer):
                (b, use), (b1, use1) = QUERY_FILLS[layer]
                load(b, use, cols(A["peer_w_q_2"][layer], 0, 512))
                for c in range(3):
                    load(b1, use1 + c, cols(A["peer_w_q_2"][layer], (c + 1) * 512, 512))

            load_queries(0)
            load(1, 11, cols(A["attn_w_qkv_2"][0], D, 512))
            sp.wait_ge(xn_done, step(3, 1))
            sp.dma_start(gain_row[:], A["ffn_norm_g_2"][1].partition_broadcast(P)).then_inc(gain_loaded, 16)
            sp.wait_ge(keys_done, ONE + 4)
            sp.dma_start(subk, A["subk"][1].rearrange("p (c n) -> p c n", c=16)).then_inc(subk_loaded, 16)
            qkv = A["attn_w_qkv_2"][0].rearrange("(k p) c -> p k c", p=P)
            with sp.Fori(0, 2) as c:
                sp.wait_ge(chunk_done[2], ONE + c + 10)
                sp.dma_start(wbuf[:, 2], qkv[:, :, bass.ds(c * 512, 512)]).then_inc(w_landed[2], 16)
            load(0, 14, cols(A["attn_w_o_2"][0], 0, 512))
            load(1, 12, cols(A["attn_w_o_2"][0], 512, 512))
            load_queries(1)
            sp.wait_ge(xn_done, step(5, 1))
            sp.dma_start(gain_row[:], A["final_norm_g_2"].partition_broadcast(P)).then_inc(gain_loaded, 16)
            for t in range(TILES):
                sp.wait_ge(xn_done, step(6, t))
                sp.dma_start(out[t * P:(t + 1) * P], xn[:, t]).then_inc(out_stored, 16)
            sp.wait_ge(out_stored, 16 * TILES)

        @block.gpsimd
        def _(pool):
            for s in counts_from_one:
                pool.sem_inc(s, ONE)
            nc.gpsimd.memset(rb[:], MASKED).then_inc(rb_cleared, 1)
            pool.wait_ge(rb_cleared, 1)
            pool.dma_start(rb[0:32, 0:24], A["rel_bias"]).then_inc(rb_loaded, 16)
            pool.dma_start(rb[0:32, 24:40], A["rel_bias_2"]).then_inc(rb_loaded, 16)
            pool.dma_start(sinks[:], A["attn_sink_2"][0].partition_broadcast(P)).then_inc(sinks_loaded, 16)
            nc.gpsimd.memset(qz[:], 0.0).then_inc(pads_zero, 1)
            pool.wait_ge(rows_copied, 2)
            pool.dma_start(bias_rows1.ap(), row1[0:HEADS1]).then_inc(rows_stored, 16)
            pool.dma_start(bias_rows2.ap(), row2[0:HEADS2]).then_inc(rows_stored, 16)
            pool.wait_ge(rows_stored, 32)
            pool.dma_start(hank1, bass.AP(bias_rows1, 0, [[1, P], [REL, HEADS1 * NG], [1, HANKEL]])).then_inc(hank1_loaded, 16)
            nc.gpsimd.memset(uT[:], 0.0).then_inc(pads_zero, 1)
            pool.wait_ge(att1_done, ONE + 16)
            pool.dma_start(wpool, A["w_pool"][0].rearrange("g c d -> c g d")).then_inc(wpool_loaded, 16)
            nc.gpsimd.memset(cu[:], 0.0).then_inc(pads_zero, 1)

            def gathers(layer):
                def half(unit, t, b):
                    n = unit * 2 + b
                    pool.wait_ge(dots_done, ONE + n)
                    pool.sem_inc(pool_waited, 1)
                    for e in range(HALF):
                        idx = expert[:, t, b * HALF + e:b * HALF + e + 1]
                        pool.indirect_dma_start(uring[:, e], None, A["peer_u_2"],
                                                bass.IndirectOffsetOnAxis(ap=idx, axis=0)).then_inc(u_landed[e], 16)
                    pool.wait_ge(v_used, ONE + n)
                    pool.sem_inc(pool_waited, 1)
                    for e in range(HALF):
                        idx = expert[:, t, b * HALF + e:b * HALF + e + 1]
                        pool.indirect_dma_start(vring[:, e], None, A["peer_v_2"],
                                                bass.IndirectOffsetOnAxis(ap=idx, axis=0)).then_inc(v_landed[e], 16)

                b, use = MIXER_FILLS[1 + layer][1]
                pool.wait_ge(chunk_done[b], ONE + use + 1)
                with pool.Fori(0, PEER_HEADS) as h:
                    for t in range(TILES):
                        unit = h * TILES + (UNITS * layer + t)
                        pool.wait_ge(expert_ready, unit + 1)
                        for b in range(2):
                            half(unit, t, b)

            gathers(0)
            pool.wait_ge(x_added, 6)
            pool.dma_start(hank2, bass.AP(bias_rows2, 0, [[1, P], [REL, HEADS2], [1, HANKEL]])).then_inc(hank2_loaded, 16)
            nc.gpsimd.memset(qz2[:], 0.0).then_inc(pads_zero, 1)
            gathers(1)

        @block.scalar
        def _(act):
            def norm(k, t):
                nc.scalar.activation(xn[:, t], x[:, t], ACT.Square, accum_out=sumsq[:, t:t + 1]).then_inc(sumsq_done, 1)
                act.wait_ge(meansq_done, step(k, t))
                nc.scalar.activation(root[:, t:t + 1], meansq[:, t:t + 1], ACT.Sqrt).then_inc(root_done, 1)

            def turned_out(n, t, gain):
                act.wait_ge(tile_turned, 2 * n + t + 1)
                src, to = tile_columns(n, t), slice(t * P, (t + 1) * P)
                if gain is None:
                    last = nc.scalar.activation(hT[:, 0:4, to], src[:, 0:4], ACT.Copy)
                else:
                    for c in range(4):
                        last = nc.scalar.activation(hT[:, c, to], src[:, c], ACT.Copy, scale=pf[:, gain + c:gain + c + 1])
                last.then_inc(tile_turned_act, 1)

            for t in range(TILES):
                act.wait_ge(x_loaded[t], 16)
                norm(0, t)
            act.wait_ge(rows_done, 1)
            nc.scalar.activation(row1[0:HEADS1, 0:2], psC[0:HEADS1, :].rearrange("p (g m) -> p g m", g=2), ACT.Copy)
            nc.scalar.activation(row1[0:HEADS1, 2], psD[0:HEADS1, 0:512], ACT.Copy).then_inc(rows_copied, 1)
            nc.scalar.activation(row2[0:HEADS2], psD[0:HEADS2, 512:1024], ACT.Copy).then_inc(rows_copied, 1)
            act.wait_ge(param_loaded, 16)
            for t in range(TILES):
                turned_out(0, t, PF_NORM)

            act.wait_ge(pads_zero, 1)
            with act.Fori(0, HEADS1 // 2) as i:
                act.wait_ge(chunk_done[0], ONE + i + 1)
                act.wait_ge(sc1_done, ONE + i * 4)
                for a in range(2):
                    r = slice(64 * a, 64 * a + 64)
                    last = nc.scalar.activation(qz[r, a], psA[r, 0:768].rearrange("p (g t) -> p g t", g=NG), ACT.Copy,
                                                scale=HD ** -0.5)
                last.then_inc(q1_copied, 1)

                def exp(u):
                    act.wait_ge(max1_done, i * 4 + u + 1)
                    act.wait_ge(probT1_done, ONE + i * 4 + max(u - 1, 0))
                    nc.scalar.activation(prob1[:, u % 2], ps[2 + u % 2][:, 0:768], ACT.Exp, bias=small[:, u:u + 1],
                                         accum_out=small[:, 4 + u:5 + u]).then_inc(exp1_done, 1)

                exp(0)
                exp(1)
                act.wait_ge(chunk_done[2], ONE + i + 1)
                act.wait_ge(av1_done, ONE + i * 4)
                nc.scalar.activation(v1[:], psA[:].rearrange("p (t c) -> p t c", t=TILES)[:, :, 0:NG * P], ACT.Copy)\
                    .then_inc(v1_copied, 1)
                exp(2)
                exp(3)

            for n, (b, src, dst) in enumerate(((1, psB, sig_a), (2, psC, sig_b))):
                act.wait_ge(chunk_done[b], ONE + 5)
                nc.scalar.activation(dst, src[:], ACT.Sigmoid).then_inc(sig_done, 1)

            for j in range(2):
                act.wait_ge(merged_done, j) if j else act.wait_ge(gates_done, 2)
                for n, (b, src, dst) in enumerate(((0, psA, sig_a), (1, psB, sig_b))):
                    act.wait_ge(chunk_done[b], ONE + 6 + j)
                    for m in range(4):
                        bias = pf[:, PF_BG + 8 * n + 4 * j + m:PF_BG + 8 * n + 4 * j + m + 1]
                        last = nc.scalar.activation(dst[:, m * SEQ:(m + 1) * SEQ], src[:, m * SEQ:(m + 1) * SEQ],
                                                    ACT.Sigmoid, bias=bias)
                    last.then_inc(merge_sig, 1)

            for t in range(TILES):
                act.wait_ge(x_added, t + 1)
                norm(1, t)
                act.wait_ge(xn_done, step(1, t))
                norm(2, t)
                turned_out(1, t, PF_CONV)

            for j in range(2):
                act.wait_ge(chunk_done[1], ONE + 9 + j)
                if j:
                    act.wait_ge(conv_done, 1)
                nc.scalar.activation(gate_c, (psB, psD)[j][:], ACT.Copy).then_inc(gc_copied, 1)

            def peer(layer):
                def tile_in(t):
                    act.wait_ge(x_added, (3, 7)[layer] + t)
                    norm(3 + 2 * layer, t)
                    turned_out((2, 5)[layer], t, None)

                def queries_out(chunk, b, use):
                    act.wait_ge(chunk_done[b], use + (ONE + 1))
                    act.wait_ge(keys_done, chunk + ONE)
                    nc.scalar.activation(pqT[:], psC[:].rearrange("p (m t) -> p m t", m=4), ACT.Copy).then_inc(pq_copied, 1)

                def scores_out(chunk):
                    act.wait_ge(keys_done, chunk + (ONE + 1))
                    act.wait_ge(topk_done, chunk * 4 + ONE)
                    nc.scalar.activation(scores[:].rearrange("p t s n -> p (t s n)"), psD[:], ACT.Copy).then_inc(scores_ready, 1)

                def softmax_exp(unit, t):
                    act.wait_ge(topk_done, unit + (ONE + 1))
                    nc.scalar.activation(gate_e, sel_v, ACT.Exp, bias=small[:, 8:9], accum_out=small[:, 9:10]).then_inc(gate_exp, 1)

                def mix(unit, t, b):
                    n = unit * 2 + b
                    e0 = b * HALF
                    act.wait_ge(dots_done, ONE + n + 1)
                    nc.scalar.activation(act_e[:, t, e0:e0 + HALF], dot[:, t, e0:e0 + HALF], ACT.Gelu).then_inc(gelu_done, 1)
                    act.wait_ge(coef_done, n + 1)
                    act.wait_ge(v_used, ONE + unit * 2)
                    for e in range(HALF):
                        nc.scalar.activation(diag[:, b, e], ident, ACT.Copy, scale=coef[:, t, e0 + e:e0 + e + 1])\
                            .then_inc(diag_done, 1)

                base = UNITS * layer
                first, (b1, use1) = QUERY_FILLS[layer]

                def chunk(c, last):
                    for k in range(4):
                        unit = c * 4 + (base + k)
                        if k == 3 and not last:
                            scores_out(c + (4 * layer + 1))
                        mix(unit, k % 2, 0)
                        if k < 3 or not last:
                            softmax_exp(unit + 1, 1 - k % 2)
                        mix(unit, k % 2, 1)
                        if k == 2 and not last:
                            queries_out(c + (4 * layer + 1), b1, c + use1)

                head_scores = psD[:].rearrange("p (t s n) -> p t s n", t=TILES, s=4)
                queries = psC[:].rearrange("p (m t) -> p m t", m=4)
                for t in range(TILES):
                    to = slice(t * P, (t + 1) * P)
                    tile_in(t)
                    act.wait_ge(first_queries, 2 * layer + t + 1)
                    act.wait_ge(keys_done, 4 * layer + ONE)
                    nc.scalar.activation(pqT[:, 0:2, to], queries[:, 0:2, to], ACT.Copy).then_inc(first_copied, 1)
                    act.wait_ge(first_keys, 2 * layer + t + 1)
                    act.wait_ge(topk_done, 16 * layer + ONE)
                    nc.scalar.activation(scores[:, t, 0:2], head_scores[:, t, 0:2], ACT.Copy).then_inc(first_scores, 1)
                    if t == 0:
                        softmax_exp(base, 0)
                act.wait_ge(chunk_done[first[0]], first[1] + (ONE + 1))
                nc.scalar.activation(pqT[:, 2:4], queries[:, 2:4], ACT.Copy).then_inc(pq_copied, 1)
                act.wait_ge(keys_done, 4 * layer + (ONE + 1))
                nc.scalar.activation(scores[:, :, 2:4], head_scores[:, :, 2:4], ACT.Copy).then_inc(scores_ready, 1)
                with act.Fori(0, 3) as c:
                    chunk(c, False)
                chunk(3, True)
                for t in range(TILES):
                    if layer == 0 and t == 1:
                        turned_out(3, 0, PF_ATT)
                    act.wait_ge(x_added, (5, 9)[layer] + t)
                    norm((4, 6)[layer], t)
                if layer == 0:
                    turned_out(3, 1, PF_ATT)

            peer(0)

            act.wait_ge(chunk_done[1], ONE + 12)
            nc.scalar.activation(kT2, psC[:, 0:512], ACT.Copy).then_inc(kv2_copied, 1)
            act.wait_ge(pads_zero, 4)
            with act.Fori(0, 2) as c:
                act.wait_ge(chunk_done[2], ONE + c + 11)
                act.wait_ge(sc2_done, ONE + c * 16)
                for i in range(8):
                    to, of = slice(64 * (i // 4), 64 * (i // 4) + 64), slice(64 * (i % 2), 64 * (i % 2) + 64)
                    last = nc.scalar.activation(qz2[to, i], psA[of, (i // 2) * SEQ:(i // 2 + 1) * SEQ], ACT.Copy,
                                                scale=HD ** -0.5)
                last.then_inc(q2_copied, 1)
                for u in range(16):
                    act.wait_ge(max2_done, c * 16 + u + 1)
                    act.wait_ge(probT2_done, ONE + c * 16 + max(u - 3, 0))
                    nc.scalar.activation(prob2[:, u % 4, 0:257], ps[2 + u // 2 % 2][:, (u % 2) * 512:(u % 2) * 512 + 257], ACT.Exp,
                                         bias=small[:, 16 + u:17 + u], accum_out=small[:, 32 + u:33 + u]).then_inc(exp2_done, 1)
            for t in range(TILES):
                turned_out(4, t, None)

            peer(1)

        @block.tensor
        def _(pe):
            mm = nc.tensor.matmul

            def turn(n, t, src):
                for c in range(KC):
                    last = nc.tensor.transpose(tile_columns(n, t)[:, c], src[:, t, c * P:(c + 1) * P], ident)
                last.then_inc(tile_turned, 1)

            def turned_in(n, t):
                pe.wait_ge(tile_turned_act, 2 * n + t + 1)
                pe.wait_ge(tile_turned_dve, 2 * n + t + 1)

            def tile_product(dst, b, m, t):
                for k in range(KC):
                    last = mm(dst[:, m * SEQ + t * P:m * SEQ + (t + 1) * P], wbuf[:, b, k, m * P:(m + 1) * P],
                              hT[:, k, t * P:(t + 1) * P], start=(k == 0), stop=(k == KC - 1))
                return last

            def mixer(n, t, j, src):
                b, use = MIXER_FILLS[n][j]
                pe.wait_ge(w_landed[b], landed_value(b, use))
                for k in range(KC):
                    last = mm(ps[j][:, t * 512:(t + 1) * 512], src[:, k, t * P:(t + 1) * P], wbuf[:, b, k],
                              start=(k == 0), stop=(k == KC - 1))
                if t == 1:
                    last.then_inc(chunk_done[b], 1)
                elif j == 1:
                    last.then_inc(mixer_out, 1)

            def columns(dst, b, use, src=hT, k0=0, k1=KC, count=True):
                pe.wait_ge(w_landed[b], landed_value(b, use))
                for m in range(4):
                    for k in range(k0, k1):
                        last = mm(dst[:, m * SEQ:(m + 1) * SEQ], wbuf[:, b, k, m * P:(m + 1) * P], src[:, k - k0],
                                  start=(k == k0), stop=(k == k1 - 1))
                if count:
                    last.then_inc(chunk_done[b], 1)

            pe.wait_ge(const_loaded, 32)
            pe.wait_ge(rb_loaded, 32)
            for n in range(4):
                heads = HEADS1 if n < NG else HEADS2
                last = mm(ps[2 + n // 2][0:heads, (n % 2) * 512:(n % 2 + 1) * 512], rb[0:33, 8 * n:8 * n + heads],
                          bucket[0:33, n * REL:(n + 1) * REL], start=True, stop=True)
            last.then_inc(rows_done, 1)

            for t in range(TILES):
                pe.wait_ge(xn_done, step(0, t))
                turn(0, t, xn)
            for t in range(TILES):
                turned_in(0, t)

            pe.wait_ge(rows_copied, 2)
            with pe.Fori(0, HEADS1 // 2) as i:
                def project(dst, b):
                    pe.wait_ge(w_landed[b], i * 48 + 48)
                    for g in range(NG):
                        for k in range(KC):
                            last = mm(dst[:, g * SEQ:(g + 1) * SEQ], wbuf[:, b, k, g * P:(g + 1) * P], hT[:, k],
                                      start=(k == 0), stop=(k == KC - 1))
                    last.then_inc(chunk_done[b], 1)

                def score(u):
                    a, t, dst = u // 2, u % 2, ps[2 + u % 2]
                    pe.wait_ge(exp1_done, ONE + i * 4 + max(u - 1, 0))
                    for g in range(NG):
                        last = mm(dst[:, g * SEQ:(g + 1) * SEQ], qz[:, a, g, t * P:(t + 1) * P], kT[:, g], start=True, stop=True)
                    last.then_inc(sc1_done, 1)

                def turn_probs(u):
                    pe.wait_ge(exp1_done, ONE + i * 4 + u + 1)
                    pe.wait_ge(probT1_copied, ONE + i * 4 + u)
                    for m in range(6):
                        last = nc.tensor.transpose(psB[:, m * P:(m + 1) * P], prob1[:, u % 2, m * P:(m + 1) * P], ident)
                    last.then_inc(probT1_done, 1)

                def times_v(u):
                    a = u // 2
                    pe.wait_ge(probT1_copied, ONE + i * 4 + u + 1)
                    pe.wait_ge(att1_done, ONE + i * 4 + max(u - 1, 0))
                    for m in range(6):
                        g, kt = m // 2, m % 2
                        last = mm(psA[:, (u % 2) * 512:(u % 2) * 512 + HD], probT1[:, u % 2, m],
                                  v1[:, kt, g * P + a * HD:g * P + a * HD + HD], start=(m == 0), stop=(m == 5))
                    last.then_inc(av1_done, 1)

                pe.wait_ge(att1_done, ONE + i * 4)
                project(psA, 0)
                pe.wait_ge(probT1_copied, ONE + i * 4)
                project(psB, 1)
                pe.wait_ge(q1_copied, i + 1)
                pe.wait_ge(k1_copied, i + 1)
                score(0)
                score(1)
                pe.wait_ge(w_landed[2], i * 48 + 48)
                for t in range(TILES):
                    for k in range(KC):
                        last = mm(psA[:, t * 512:t * 512 + NG * P], hT[:, k, t * P:(t + 1) * P], wbuf[:, 2, k, 0:NG * P],
                                  start=(k == 0), stop=(k == KC - 1))
                last.then_inc(chunk_done[2], 1)
                turn_probs(0)
                score(2)
                turn_probs(1)
                pe.wait_ge(v1_copied, i + 1)
                times_v(0)
                score(3)
                turn_probs(2)
                times_v(1)
                turn_probs(3)
                times_v(2)
                times_v(3)

            pe.wait_ge(att1_done, ONE + 16)
            columns(psA, 0, 4)
            pe.wait_ge(probT1_copied, ONE + 16)
            columns(psB, 1, 4)
            pe.wait_ge(exp1_done, ONE + 16)
            columns(psC, 2, 4)
            for m in range(4):
                for t in range(TILES):
                    last = nc.tensor.transpose(psD[:, m * SEQ + t * P:m * SEQ + (t + 1) * P], att1[:, t, m * P:(m + 1) * P], ident)
            last.then_inc(att1_turned, 1)
            pe.wait_ge(pooled_done, 1)
            pe.wait_ge(wpool_loaded, 16)
            for g in range(POOL_GROUPS):
                last = mm(psA[:, g * SEQ:(g + 1) * SEQ], wpool[:, g], pooled[:, g], start=True, stop=True)
            last.then_inc(mixed_done, 1)
            for j in range(2):
                if j == 0:
                    pe.wait_ge(ya_done, 1)
                    pe.wait_ge(gates_done, 2)
                else:
                    pe.wait_ge(merge_sig, 2)
                columns(psA, 0, 5 + j)
                columns(psB, 1, 5 + j)
                if j == 0:
                    pe.wait_ge(yb_done, 1)
                else:
                    pe.wait_ge(merged_done, 1)
                columns(psC, 2, 5 + j, src=yaT, k0=0, k1=4, count=False)
                columns(psD, 2, 5 + j, src=ybT, k0=4, k1=8)
            pe.wait_ge(merge_sig, 4)
            pe.wait_ge(merged_done, 2)
            for t in range(TILES):
                for j in range(2):
                    mixer(0, t, j, merged)

            pe.wait_ge(xn_done, step(2, 0))
            turn(1, 0, xn)
            turned_in(1, 0)
            pe.wait_ge(x_added, 2)
            for t in range(TILES):
                if t:
                    pe.wait_ge(xn_done, step(2, 1))
                    turn(1, 1, xn)
                    turned_in(1, 1)
                for b, dst in ((0, psA), (1, psB)):
                    pe.wait_ge(w_landed[b], landed_value(b, 8))
                    for m in range(4):
                        last = tile_product(dst, b, m, t)
                    if t:
                        last.then_inc(chunk_done[b], 1)
            columns(psC, 2, 7)
            columns(psD, 1, 9)
            pe.wait_ge(conv_done, 1)
            columns(psC, 2, 8)
            columns(psA, 0, 9)
            pe.wait_ge(conv_done, 2)

            def peer(layer):
                (b0, use0), (b1, use1) = QUERY_FILLS[layer]
                mixed, n = (cT, hT)[layer], (2, 5)[layer]

                def keys(chunk, tiles=range(TILES), halves=range(4)):
                    for t in tiles:
                        for m in halves:
                            last = mm(psD[:, t * 512 + m * NKEYS:t * 512 + (m + 1) * NKEYS], pqT[:, m, t * P:(t + 1) * P],
                                      next_keys(chunk, m), start=True, stop=True)
                    return last

                def next_keys(chunk, m):
                    c = chunk - 4 * layer
                    return subk[:, m] if isinstance(c, int) else arena[:, bass.ds(c * (4 * NKEYS) + (SUBK + m * NKEYS), NKEYS)]

                def first_head(t):
                    tile_product(psC, b0, 0, t)
                    tile_product(psC, b0, 1, t).then_inc(first_queries, 1)
                    pe.wait_ge(subk_loaded, 16 * (layer + 1))
                    pe.wait_ge(first_copied, 2 * layer + t + 1)
                    if layer:
                        pe.wait_ge(scores_ready, 4 * layer)
                    keys(4 * layer, (t,), (0, 1)).then_inc(first_keys, 1)

                mixer(1 + layer, 0, 0, mixed)
                mixer(1 + layer, 0, 1, mixed)
                mixer(1 + layer, 1, 0, mixed)
                pe.wait_ge(xn_done, step(3 + 2 * layer, 0))
                turn(n, 0, xn)
                turned_in(n, 0)
                pe.wait_ge(w_landed[b0], landed_value(b0, use0))
                first_head(0)
                mixer(1 + layer, 1, 1, mixed)
                tile_product(psC, b0, 2, 0)
                tile_product(psC, b0, 3, 0)
                pe.wait_ge(x_added, (4, 8)[layer])
                pe.wait_ge(xn_done, step(3 + 2 * layer, 1))
                turn(n, 1, xn)
                turned_in(n, 1)
                first_head(1)
                tile_product(psC, b0, 2, 1)
                tile_product(psC, b0, 3, 1).then_inc(chunk_done[b0], 1)
                pe.wait_ge(pq_copied, 4 * layer + 1)
                keys(4 * layer, range(TILES), (2, 3)).then_inc(keys_done, 1)
                pe.wait_ge(zeros_ready, 1)
                for t in range(TILES):
                    for s in range(2):
                        mm(ps[t][:, s * 512:(s + 1) * 512], zeros, xn[:, 0, 0:512], start=True, stop=False,
                           skip_group_check=True)

                def chunk(c, last):
                    for k in range(4):
                        for b in range(2):
                            n = c * 8 + (2 * UNITS * layer + 2 * k + b)
                            m = 2 * k + b - 2
                            if not last and 0 <= m < 4:
                                if m == 0:
                                    pe.wait_ge(w_landed[b1], c * 16 + landed_value(b1, use1))
                                    pe.wait_ge(pq_copied, c + (4 * layer + 1))
                                for kc in range(KC):
                                    mq = mm(psC[:, m * SEQ:(m + 1) * SEQ], wbuf[:, b1, kc, m * P:(m + 1) * P], hT[:, kc],
                                            start=(kc == 0), stop=(kc == KC - 1))
                                if m == 3:
                                    mq.then_inc(chunk_done[b1], 1)
                            if not last and k == 3 and b == 0:
                                pe.wait_ge(pq_copied, c + (4 * layer + 2))
                                pe.wait_ge(scores_ready, c + (4 * layer + 1))
                                keys(c + (4 * layer + 1)).then_inc(keys_done, 1)
                            for e in range(HALF):
                                pe.wait_ge(v_landed[e], n * 16 + 16)
                                pe.wait_ge(diag_done, n * HALF + (e + 1))
                                for s in range(2):
                                    mv = mm(ps[k % 2][:, s * 512:(s + 1) * 512], diag[:, b, e], vring[:, e, s * 512:(s + 1) * 512],
                                            start=False, stop=False, skip_group_check=True)
                            mv.then_inc(v_used, 1)

                with pe.Fori(0, 3) as c:
                    chunk(c, False)
                chunk(3, True)

            peer(0)

            pe.wait_ge(w_landed[1], landed_value(1, 11))
            for t in range(TILES):
                pe.wait_ge(xn_done, step(4, t))
                turn(3, t, xn)
                turned_in(3, t)
                for m in range(2):
                    tile_product(psC, 1, m, t)
                for k in range(KC):
                    last = mm(psC[:, 512 + t * 256:512 + (t + 1) * 256], hT[:, k, t * P:(t + 1) * P], wbuf[:, 1, k, 256:512],
                              start=(k == 0), stop=(k == KC - 1))
            last.then_inc(chunk_done[1], 1)
            pe.wait_ge(x_added, 6)
            pe.wait_ge(kv2_copied, 1)
            pe.wait_ge(v2_copied, 1)
            pe.wait_ge(sinks_loaded, 16)
            with pe.Fori(0, 2) as c:
                pe.wait_ge(w_landed[2], c * 16 + landed_value(2, 10))
                pe.wait_ge(att2_done, ONE + c * 16)
                for m in range(4):
                    for k in range(KC):
                        last = mm(psA[:, m * SEQ:(m + 1) * SEQ], wbuf[:, 2, k, m * P:(m + 1) * P], hT[:, k],
                                  start=(k == 0), stop=(k == KC - 1))
                last.then_inc(chunk_done[2], 1)
                pe.wait_ge(q2_copied, c + 1)

                def score(u):
                    i, t = u // 2, u % 2
                    dst = ps[2 + u // 2 % 2][:, (u % 2) * 512:(u % 2) * 512 + 257]
                    pe.wait_ge(exp2_done, ONE + c * 16 + max(u - 3, 0))
                    mm(dst[:, 256:257], ident, sinks[:, bass.ds(c * 8 + i, 1)], start=True, stop=True)
                    mm(dst[:, 0:256], qz2[:, i, t * P:(t + 1) * P], kT2[:, bass.ds(c * SEQ, SEQ)], start=True, stop=True).then_inc(sc2_done, 1)

                def turn_probs(u):
                    pe.wait_ge(exp2_done, ONE + c * 16 + u + 1)
                    pe.wait_ge(probT2_copied, ONE + c * 16 + max(u - 1, 0))
                    for kt in range(2):
                        last = nc.tensor.transpose(psB[:, (u % 2) * 512 + kt * P:(u % 2) * 512 + (kt + 1) * P],
                                                   prob2[:, u % 4, kt * P:(kt + 1) * P], ident)
                    last.then_inc(probT2_done, 1)

                def times_v(u):
                    i = u // 2
                    pe.wait_ge(probT2_copied, ONE + c * 16 + u + 1)
                    pe.wait_ge(att2_done, ONE + c * 16 + max(u - 1, 0))
                    for kt in range(2):
                        last = mm(psA[:, (u % 2) * 512:(u % 2) * 512 + HD], probT2[:, u % 4, kt],
                                  v2[:, kt, bass.ds(c * P + (i // 4) * HD, HD)], start=(kt == 0), stop=(kt == 1))
                    last.then_inc(av2_done, 1)

                for s in range(16 + 3):
                    if s < 16:
                        score(s)
                    if 0 <= s - 2 < 16:
                        turn_probs(s - 2)
                    if 0 <= s - 3 < 16:
                        times_v(s - 3)
            pe.wait_ge(att2_done, ONE + 32)
            for t in range(TILES):
                turn(4, t, att2)
            for t in range(TILES):
                turned_in(4, t)
            peer(1)

        @block.vector
        def _(dve):
            class Chain:
                first, n = 0, 0

                def link(self, ins):
                    self.n += 1
                    ins.then_inc(dve_step, 1)
                    dve.wait_ge(dve_step, self.first + self.n)

                def loop(self, i, per):
                    self.before, self.first, self.n, self.per = self.first + self.n, i * per + (self.first + self.n), 0, per

                def end(self, times):
                    assert self.n == self.per, self.n
                    self.first, self.n = self.before + times * self.per, 0

            chain = Chain()
            link = chain.link

            def one_over_root(n, tiles):
                dve.wait_ge(meansq_done, n)
                dve.wait_ge(root_done, n)
                m, y, z = meansq[:, tiles], root[:, tiles], rinv[:, tiles]
                link(nc.vector.reciprocal(y, y))
                link(nc.vector.tensor_tensor(z, y, y, ALU.mult))
                link(nc.vector.tensor_tensor(z, z, m, ALU.mult))
                link(nc.vector.tensor_scalar(z, z, -0.5, 1.5, ALU.mult, ALU.add))
                link(nc.vector.tensor_tensor(z, z, y, ALU.mult))

            def norm(k, t, gains, dst):
                dve.wait_ge(sumsq_done, step(k, t))
                nc.vector.tensor_scalar(meansq[:, t:t + 1], sumsq[:, t:t + 1], 1.0 / D, EPS, ALU.mult, ALU.add)\
                    .then_inc(meansq_done, 1)
                dve.wait_ge(meansq_done, step(k, t))
                dve.wait_ge(root_done, step(k, t))
                m, y, z = meansq[:, t:t + 1], root[:, t:t + 1], rinv[:, t:t + 1]
                link(nc.vector.reciprocal(y, y))
                link(nc.vector.tensor_tensor(z, y, y, ALU.mult))
                link(nc.vector.tensor_tensor(z, z, m, ALU.mult))
                link(nc.vector.tensor_scalar(z, z, -0.5, 1.5, ALU.mult, ALU.add))
                link(nc.vector.tensor_tensor(z, z, y, ALU.mult))
                if gains is None:
                    nc.vector.tensor_scalar(dst[:, t], x[:, t], z, None, ALU.mult).then_inc(xn_done, 1)
                else:
                    dve.wait_ge(gain_loaded, 16 * gains)
                    nc.vector.scalar_tensor_tensor(out=dst[:, t], in0=x[:, t], scalar=z, in1=gain_row[:],
                                                   op0=ALU.mult, op1=ALU.mult).then_inc(xn_done, 1)

            def turned_out(n, t, gain):
                dve.wait_ge(tile_turned, 2 * n + t + 1)
                src, to = tile_columns(n, t), slice(t * P, (t + 1) * P)
                if gain is None:
                    last = nc.vector.tensor_copy(hT[:, 4:8, to], src[:, 4:8])
                else:
                    for c in range(4, 8):
                        last = nc.vector.tensor_scalar(hT[:, c, to], src[:, c], pf[:, gain + c:gain + c + 1], None, ALU.mult)
                last.then_inc(tile_turned_dve, 1)

            def residual(n, t):
                if t == 0:
                    dve.wait_ge(mixer_out, n + 1)
                else:
                    for b, use in MIXER_FILLS[n]:
                        dve.wait_ge(chunk_done[b], ONE + use + 1)
                for j in range(2):
                    dst = x[:, t, j * 512:(j + 1) * 512]
                    last = nc.vector.tensor_tensor(dst, ps[j][:, t * 512:(t + 1) * 512], dst, ALU.add)
                last.then_inc(x_added, 1)

            for t in range(TILES):
                norm(0, t, None, xn)
            dve.wait_ge(param_loaded, 16)
            for t in range(TILES):
                turned_out(0, t, PF_NORM)

            def tile_of_bias(first, heads, t):
                tables = arena[:, bass.ds(first, heads * HANKEL)].rearrange("p (h m) -> p h m", h=heads)
                return tables[:, :, P * (1 - t):P * (1 - t) + SEQ]

            dve.wait_ge(hank1_loaded, 16)
            link(nc.vector.tensor_copy(bias1, hank1[:, :, ::-1]))

            with dve.Fori(0, HEADS1 // 2) as i:
                chain.loop(i, 8)
                dve.wait_ge(chunk_done[1], ONE + i + 1)
                dve.wait_ge(sc1_done, ONE + i * 4)
                nc.vector.tensor_copy(kT[:], psB[:, 0:768].rearrange("p (g t) -> p g t", g=NG)).then_inc(k1_copied, 1)

                def row_max(u):
                    dve.wait_ge(sc1_done, ONE + i * 4 + u + 1)
                    biased = ps[2 + u % 2][:, 0:768].rearrange("p (g t) -> p g t", g=NG)
                    link(nc.vector.tensor_tensor(biased, biased, tile_of_bias(i * (6 * HANKEL) + u // 2 * NG * HANKEL, NG, u % 2),
                                                 ALU.add))
                    nc.vector.tensor_reduce(small[:, u:u + 1], ps[2 + u % 2][:, 0:768], AX_X, ALU.max, negate=True)\
                        .then_inc(max1_done, 1)

                def copy_probs(u):
                    dve.wait_ge(probT1_done, ONE + i * 4 + u + 1)
                    dve.wait_ge(av1_done, ONE + i * 4 + max(u - 1, 0))
                    nc.vector.tensor_copy(probT1[:, u % 2], psB[:, 0:768].rearrange("p (m t) -> p m t", m=6))\
                        .then_inc(probT1_copied, 1)

                def output(u):
                    a, t = u // 2, u % 2
                    link(nc.vector.reciprocal(small[:, 10 + u:11 + u], small[:, 4 + u:5 + u]))
                    dve.wait_ge(av1_done, ONE + i * 4 + u + 1)
                    nc.vector.tensor_scalar(att1[:, t, bass.ds(i * P + a * HD, HD)], psA[:, (u % 2) * 512:(u % 2) * 512 + HD],
                                            small[:, 10 + u:11 + u], None, ALU.mult).then_inc(att1_done, 1)

                row_max(0)
                row_max(1)
                copy_probs(0)
                row_max(2)
                copy_probs(1)
                output(0)
                row_max(3)
                copy_probs(2)
                output(1)
                copy_probs(3)
                output(2)
                output(3)
            chain.end(HEADS1 // 2)

            nc.vector.memset(zeros, 0.0).then_inc(zeros_ready, 1)
            dve.wait_ge(pads_zero, 2)
            dve.wait_ge(chunk_done[0], ONE + 5)
            link(nc.vector.tensor_copy(uT[:, :, PAD:PAD + SEQ], psA[:].rearrange("p (g t) -> p g t", g=4)))

            def window(dst, src, g, lo, hi, shift):
                left = 1 if shift == 0 else shift
                link(nc.vector.tensor_tensor(dst[:, g:4, PAD + lo:PAD + hi], src[:, g:4, PAD + lo - left:PAD + hi - left],
                                             src[:, g:4, PAD + lo + shift:PAD + hi + shift], ALU.add))

            window(win2, uT, 0, -7, SEQ + 7, 0)
            window(win4, win2, 1, -6, SEQ + 6, 1)
            window(win8, win4, 2, -4, SEQ + 4, 2)
            window(win2, win8, 3, 0, SEQ, 4)
            sums = (win2, win4, win8, win2)
            for g in range(4):
                last = nc.vector.tensor_tensor(pooled[:, g], sums[g][:, g, PAD:PAD + SEQ], inv_count[:, g], ALU.mult)
            link(last)
            nc.vector.tensor_tensor(pooled[:], pooled[:], uT[:, :, PAD:PAD + SEQ], ALU.subtract).then_inc(pooled_done, 1)

            dve.wait_ge(sig_done, 1)
            nc.vector.tensor_tensor(gate_a, psB[:], sig_a, ALU.mult).then_inc(gates_done, 1)
            dve.wait_ge(sig_done, 2)
            nc.vector.tensor_tensor(gate_b, psC[:], sig_b, ALU.mult).then_inc(gates_done, 1)
            dve.wait_ge(gates_done, 2)
            dve.wait_ge(att1_turned, 1)
            nc.vector.tensor_tensor(ybT[:].rearrange("p m t -> p (m t)"), psD[:], gate_b, ALU.mult).then_inc(yb_done, 1)
            dve.wait_ge(mixed_done, 1)
            for g in range(POOL_GROUPS):
                last = nc.vector.scalar_tensor_tensor(out=yaT[:, g], in0=psA[:, g * SEQ:(g + 1) * SEQ],
                                                      scalar=pf[:, PF_POOL + g:PF_POOL + g + 1],
                                                      in1=gate_a[:, g * SEQ:(g + 1) * SEQ], op0=ALU.mult, op1=ALU.mult)
            last.then_inc(ya_done, 1)
            for j in range(2):
                dve.wait_ge(merge_sig, 2 * j + 2)
                dve.wait_ge(chunk_done[2], ONE + 6 + j)
                nc.vector.tensor_tensor(prod_a, psC[:], sig_a, ALU.mult)
                link(nc.vector.tensor_tensor(prod_b, psD[:], sig_b, ALU.mult))
                nc.vector.tensor_tensor(merged[:, 4 * j:4 * j + 4].rearrange("p m t -> p (m t)"), prod_a, prod_b, ALU.add)\
                    .then_inc(merged_done, 1)
            dve.wait_ge(merged_done, 2)
            for t in range(TILES):
                residual(0, t)
                norm(1, t, 1, x)
                dve.wait_ge(xn_done, step(1, t))
                norm(2, t, None, xn)
                turned_out(1, t, PF_CONV)

            dve.wait_ge(pads_zero, 3)
            for j in range(2):
                dve.wait_ge(gc_copied, j + 1)
                dve.wait_ge(chunk_done[2], ONE + 8 + j)
                link(nc.vector.tensor_tensor(cu[:, :, 1:1 + SEQ], psC[:].rearrange("p (m t) -> p m t", m=4),
                                             gate_c.rearrange("p (m t) -> p m t", m=4), ALU.mult))
                for tap in range(3):
                    for m in range(4):
                        w = pf[:, PF_CW + tap * KC + 4 * j + m:PF_CW + tap * KC + 4 * j + m + 1]
                        if tap == 0:
                            last = nc.vector.tensor_scalar(cacc[:, m], cu[:, m, 0:SEQ], w, None, ALU.mult)
                        else:
                            last = nc.vector.scalar_tensor_tensor(out=cacc[:, m], in0=cu[:, m, tap:tap + SEQ], scalar=w,
                                                                  in1=cacc[:, m], op0=ALU.mult, op1=ALU.add)
                    link(last)
                dve.wait_ge(chunk_done[0], ONE + 9 + j)
                nc.vector.tensor_tensor(cT[:, 4 * j:4 * j + 4], psA[:].rearrange("p (m t) -> p m t", m=4), cacc[:], ALU.mult)\
                    .then_inc(conv_done, 1)
                dve.wait_ge(conv_done, j + 1)

            def peer(layer):
                def tile_in(t):
                    residual(1 + layer, t)
                    norm(3 + 2 * layer, t, 2 + layer, xn)
                    turned_out((2, 5)[layer], t, None)

                def apart():
                    dve.sem_inc(dve_waited, 1)

                def linked(ins):
                    link(ins)
                    apart()

                def top16(values, indices, src, n):
                    for p in range(n):
                        last = nc.vector.max(values(p, 0), src(p))
                    linked(last)
                    for p in range(n):
                        last = nc.vector.max_index(indices(p, 0), values(p, 0), src(p))
                    linked(last)
                    for p in range(n):
                        last = nc.vector.match_replace(src(p), values(p, 0), src(p), LOWEST)
                    linked(last)
                    for p in range(n):
                        last = nc.vector.max(values(p, 1), src(p))
                    linked(last)
                    for p in range(n):
                        last = nc.vector.max_index(indices(p, 1), values(p, 1), src(p))
                    linked(last)

                def topk(unit, t, head):
                    top16(lambda p, r: top_v[:, p, 8 * r:8 * r + 8], lambda p, r: top_i[:, p, 8 * r:8 * r + 8],
                          lambda p: scores[:, t, 2 * head + p], 2)
                    grid = cand.rearrange("p (a b) -> p a b", a=TOPK)
                    linked(nc.vector.tensor_tensor(grid, top_v[:, 0].unsqueeze(2).to_broadcast([P, TOPK, TOPK]),
                                                 top_v[:, 1].unsqueeze(1).to_broadcast([P, TOPK, TOPK]), ALU.add))
                    top16(lambda p, r: sel_v[:, 8 * r:8 * r + 8], lambda p, r: sel_p[:, 8 * r:8 * r + 8], lambda p: cand, 1)
                    nc.vector.tensor_scalar(small[:, 8:9], sel_v[:, 0:1], -1.0, None, ALU.mult).then_inc(topk_done, 1)
                    nc.vector.tensor_scalar(sel_i, sel_p, 4, None, ALU.logical_shift_right)
                    link(nc.vector.tensor_scalar(sel_j, sel_p, 15, None, ALU.bitwise_and))
                    for p, sel in enumerate((sel_i, sel_j)):
                        last = nc.vector.tensor_tensor(onehot[:, p], sel.unsqueeze(2).to_broadcast([P, TOPK, TOPK]),
                                                       iota16.unsqueeze(1).to_broadcast([P, TOPK, TOPK]), ALU.is_equal)
                    link(last)
                    for p in range(2):
                        last = nc.vector.tensor_tensor(onehot[:, p], onehot[:, p],
                                                       top_i[:, p].unsqueeze(1).to_broadcast([P, TOPK, TOPK]), ALU.mult)
                    link(last)
                    link(nc.vector.tensor_reduce(key_ij[:], onehot[:], AX_X, ALU.add))
                    link(nc.vector.tensor_scalar(key_ij[:, 0], key_ij[:, 0], float(NKEYS), float(EXPERTS * layer), ALU.mult, ALU.add))
                    dve.wait_ge(v_used, ONE + 2 * unit - 2 if not isinstance(unit, int) else max(2 * unit - 2, 0))
                    nc.vector.tensor_tensor(expert[:, t], key_ij[:, 0], key_ij[:, 1], ALU.add).then_inc(expert_ready, 1)
                    dve.wait_ge(gate_exp, unit + 1)
                    link(nc.vector.reciprocal(small[:, 14:15], small[:, 9:10]))
                    link(nc.vector.tensor_scalar(gate[:, t], gate_e, small[:, 14:15], None, ALU.mult))

                STEPS = 18

                def dots(unit, t, b):
                    n = unit * 2 + b
                    for e in range(HALF):
                        dve.wait_ge(u_landed[e], n * 16 + 16)
                        last = nc.vector.tensor_tensor_reduce(out=uring[:, e], in0=xn[:, t], in1=uring[:, e], scale=1.0,
                                                              scalar=0.0, op0=ALU.mult, op1=ALU.add,
                                                              accum_out=dot[:, t, b * HALF + e:b * HALF + e + 1])
                    last.then_inc(dots_done, 1)

                def coefs(unit, t, b):
                    n = unit * 2 + b
                    dve.wait_ge(gelu_done, n + 1)
                    e = slice(b * HALF, (b + 1) * HALF)
                    nc.vector.tensor_tensor(coef[:, t, e], act_e[:, t, e], gate[:, t, e], ALU.mult).then_inc(coef_done, 1)

                base = UNITS * layer

                def chunk(c, last):
                    for k in range(4):
                        unit = c * 4 + (base + k)
                        dots(unit, k % 2, 0)
                        coefs(unit, k % 2, 0)
                        if k == 0:
                            dve.wait_ge(first_scores, 2 * layer + 2)
                            apart()
                            topk(unit + 1, 1, 0)
                        elif k == 1:
                            dve.wait_ge(scores_ready, c + (4 * layer + 1))
                            apart()
                            topk(unit + 1, 0, 1)
                        elif k == 2:
                            topk(unit + 1, 1, 1)
                        elif not last:
                            dve.wait_ge(scores_ready, c + (4 * layer + 2))
                            apart()
                            topk(unit + 1, 0, 0)
                        dots(unit, k % 2, 1)
                        coefs(unit, k % 2, 1)

                tile_in(0)
                dve.wait_ge(first_scores, 2 * layer + 1)
                apart()
                topk(base, 0, 0)
                tile_in(1)
                with dve.Fori(0, 3) as c:
                    chain.loop(c, 4 * STEPS)
                    chunk(c, False)
                chain.end(3)
                chunk(3, True)
                for t in range(TILES):
                    dve.wait_ge(v_used, ONE + 2 * UNITS * (layer + 1) - 2 * (1 - t))
                    nc.vector.tensor_tensor(x[:, t], ps[t][:], x[:, t], ALU.add).then_inc(x_added, 1)
                    if layer == 0:
                        if t == 1:
                            turned_out(3, 0, PF_ATT)
                        norm(4, t, None, xn)
                    else:
                        norm(6, t, 4, xn)
                if layer == 0:
                    turned_out(3, 1, PF_ATT)

            peer(0)

            dve.wait_ge(hank2_loaded, 16)
            link(nc.vector.tensor_copy(bias2, hank2[:, :, ::-1]))
            dve.wait_ge(chunk_done[1], ONE + 12)
            nc.vector.tensor_copy(v2[:], psC[:, 512:1024].rearrange("p (t c) -> p t c", t=TILES)).then_inc(v2_copied, 1)
            with dve.Fori(0, 2) as c:
                chain.loop(c, 32)

                def row_max(u):
                    dve.wait_ge(sc2_done, ONE + c * 16 + u + 1)
                    biased = ps[2 + u // 2 % 2][:, (u % 2) * 512:(u % 2) * 512 + 256].rearrange("p (h t) -> p h t", h=1)
                    link(nc.vector.tensor_tensor(biased, biased, tile_of_bias(c * (8 * HANKEL) + u // 2 * HANKEL, 1, u % 2), ALU.add))
                    nc.vector.tensor_reduce(small[:, 16 + u:17 + u], ps[2 + u // 2 % 2][:, (u % 2) * 512:(u % 2) * 512 + 257],
                                            AX_X, ALU.max, negate=True).then_inc(max2_done, 1)

                def copy_probs(u):
                    dve.wait_ge(probT2_done, ONE + c * 16 + u + 1)
                    dve.wait_ge(av2_done, ONE + c * 16 + max(u - 3, 0))
                    nc.vector.tensor_copy(probT2[:, u % 4], psB[:, (u % 2) * 512:(u % 2) * 512 + 256].rearrange(
                        "p (m t) -> p m t", m=2)).then_inc(probT2_copied, 1)

                def output(u):
                    i, t = u // 2, u % 2
                    link(nc.vector.reciprocal(small[:, 48 + u % 2:49 + u % 2], small[:, 32 + u:33 + u]))
                    dve.wait_ge(av2_done, ONE + c * 16 + u + 1)
                    nc.vector.tensor_scalar(att2[:, t, bass.ds(c * 512 + i * HD, HD)], psA[:, (u % 2) * 512:(u % 2) * 512 + HD],
                                            small[:, 48 + u % 2:49 + u % 2], None, ALU.mult).then_inc(att2_done, 1)

                for s in range(16 + 3):
                    if s < 16:
                        row_max(s)
                    if 0 <= s - 2 < 16:
                        copy_probs(s - 2)
                    if 0 <= s - 3 < 16:
                        output(s - 3)
            chain.end(2)
            for t in range(TILES):
                turned_out(4, t, None)
            peer(1)


def kernel(**inputs):
    import concourse.bacc as bacc
    from concourse.bass_utils import run_bass_kernel_spmd

    def raw(name):
        return np.ascontiguousarray(inputs[name])

    def feature_columns(v):
        return np.ascontiguousarray(np.reshape(v, (-1, P)).T)

    arrays = {n: raw(n) for n in ("x", "w_in", "rel_bias", "w_pool", "w_proj_a", "w_proj_b", "w_out", "final_gain",
                                  "conv_w_in_2", "conv_w_out_2", "attn_w_qkv_2", "attn_sink_2", "attn_w_o_2",
                                  "rel_bias_2", "ffn_norm_g_2", "peer_w_q_2", "final_norm_g_2")}
    for n in ("peer_u_2", "peer_v_2"):
        arrays[n] = raw(n).reshape(2 * EXPERTS, D)
    arrays["subk"] = np.ascontiguousarray(raw("peer_subkeys_2").transpose(0, 4, 1, 2, 3).reshape(2, P, 16 * NKEYS))
    arrays["pf"] = np.concatenate([feature_columns(raw(n)) for n in (
        "norm_gain", "conv_norm_g_2", "attn_norm_g_2", "pool_scale", "b_gate", "conv_w_2")], axis=1)
    arrays["const"] = constants()
    arrays["bucket"] = bucket_table()

    nc = bacc.Bacc("TRN2", target_bir_lowering=False, num_devices=1)
    aps = {n: nc.dram_tensor(f"in_{n}", a.shape, mybir.dt.from_np(a.dtype), kind="ExternalInput").ap()
           for n, a in arrays.items()}
    out = nc.dram_tensor("out", (SEQ, D), F32, kind="ExternalOutput").ap()
    build(nc, aps, out)
    r = run_bass_kernel_spmd(nc, [{f"in_{n}": a for n, a in arrays.items()}], core_ids=[0])
    return r.results[0]["out"].reshape(1, SEQ, D)
```
